# Optimizing a Trainium2 kernel written in Bass

```python
import math
import jax, jax.numpy as jnp
from jax import lax
import numpy as np

D_MODEL = 2048
BATCH = 1
SEQ = 256
DEPTH = 2

CHUNK = 64
N_MIXERS = 2
N_ATTN_LAYERS = (DEPTH + 1) // 2
N_CONV_LAYERS = DEPTH // 2
HEAD_DIM = 64
N_Q_HEADS = D_MODEL // HEAD_DIM
N_KV_HEADS = 8
GROUPS = N_Q_HEADS // N_KV_HEADS
WINDOW = 128
WINDOW_CHUNKS = WINDOW // CHUNK
ROPE_THETA = 500000.0
ROT_DIM = HEAD_DIM // 4
ROT_HALF = ROT_DIM // 2
CONV_WIDTH = 31
D_FF = 5632
FFN_CONV_WIDTH = 3
LN_EPS = 1e-5
ALPHA = (2.0 * DEPTH) ** 0.25
BETA = (8.0 * DEPTH) ** -0.25

kernel_name = "hybrid_swa_sink_conformer_convffn_deepnorm"

def layer_norm(x, g, b):
    xf = x.astype(jnp.float32)
    mean = jnp.mean(xf, axis=-1, keepdims=True)
    var = jnp.mean(jnp.square(xf - mean), axis=-1, keepdims=True)
    y = (xf - mean) * lax.rsqrt(var + LN_EPS) * g.astype(jnp.float32) + b.astype(jnp.float32)
    return y.astype(x.dtype)

def causal_depthwise_conv(h, w):
    k = w.shape[0]
    return lax.conv_general_dilated(
        h, w[:, None, :].astype(h.dtype), window_strides=(1,), padding=[(k - 1, 0)],
        dimension_numbers=("NWC", "WIO", "NWC"), feature_group_count=h.shape[-1])

def rotary_tables(seq_len, dtype):
    inv_freq = ROPE_THETA ** (-jnp.arange(0, ROT_DIM, 2, dtype=jnp.float32) / ROT_DIM)
    ang = jnp.arange(seq_len, dtype=jnp.float32)[:, None] * inv_freq[None, :]
    return jnp.cos(ang).astype(dtype), jnp.sin(ang).astype(dtype)

def apply_partial_rotary(t, cos, sin):
    x1 = t[..., :ROT_HALF]
    x2 = t[..., ROT_HALF:ROT_DIM]
    return jnp.concatenate([x1 * cos - x2 * sin, x2 * cos + x1 * sin, t[..., ROT_DIM:]], axis=-1)

def chunk_band(t):
    b, s = t.shape[:2]
    n_chunks = s // CHUNK
    tc = t.reshape(b, n_chunks, CHUNK, *t.shape[2:])
    padded = jnp.pad(tc, ((0, 0), (WINDOW_CHUNKS - 1, 0), (0, 0), (0, 0), (0, 0)))
    return jnp.concatenate([padded[:, j:j + n_chunks] for j in range(WINDOW_CHUNKS)], axis=2)

def sliding_window_sink_attention(h, wq, wk, wv, wo, sinks):
    b, s, _ = h.shape
    n_chunks = s // CHUNK
    q = (h @ wq).reshape(b, s, N_KV_HEADS, GROUPS, HEAD_DIM)
    k = (h @ wk).reshape(b, s, N_KV_HEADS, HEAD_DIM)
    v = (h @ wv).reshape(b, s, N_KV_HEADS, HEAD_DIM)
    cos, sin = rotary_tables(s, h.dtype)
    q = apply_partial_rotary(q, cos[None, :, None, None, :], sin[None, :, None, None, :])
    k = apply_partial_rotary(k, cos[None, :, None, :], sin[None, :, None, :])

    qc = q.reshape(b, n_chunks, CHUNK, N_KV_HEADS, GROUPS, HEAD_DIM)
    kb = chunk_band(k)
    vb = chunk_band(v)

    scale = HEAD_DIM ** -0.5
    scores = jnp.einsum("bcqngd,bcknd->bngcqk", qc.astype(jnp.float32),
                        kb.astype(jnp.float32)) * scale
    key_chunk = (jnp.arange(n_chunks)[:, None]
                 + (jnp.arange(WINDOW_CHUNKS * CHUNK) // CHUNK)[None, :]
                 - (WINDOW_CHUNKS - 1))
    valid = key_chunk >= 0
    scores = jnp.where(valid[None, None, None, :, None, :], scores, -jnp.inf)

    sink = sinks.astype(jnp.float32).reshape(1, N_KV_HEADS, GROUPS, 1, 1, 1)
    m = jnp.maximum(jnp.max(scores, axis=-1, keepdims=True), sink)
    p = jnp.exp(scores - m)
    probs = p / (jnp.sum(p, axis=-1, keepdims=True) + jnp.exp(sink - m))

    out = jnp.einsum("bngcqk,bcknd->bcqngd", probs.astype(vb.dtype), vb)
    return out.reshape(b, s, N_Q_HEADS * HEAD_DIM) @ wo

def conformer_conv_module(h, w_in, dw, norm_g, norm_b, w_out):
    u = h @ w_in
    a, g = jnp.split(u, 2, axis=-1)
    u = a * jax.nn.sigmoid(g)
    u = causal_depthwise_conv(u, dw)
    u = jax.nn.silu(layer_norm(u, norm_g, norm_b))
    return u @ w_out

def conv_ffn(h, w_up, dw, w_down):
    u = causal_depthwise_conv(h @ w_up, dw)
    gate, val = jnp.split(u, 2, axis=-1)
    return (jax.nn.silu(gate) * val) @ w_down

def setup_inputs(seed: int = 0) -> dict:
    key = jax.random.key(seed)
    ks = jax.random.split(key, 20)
    f32 = jnp.float32
    d, hd = D_MODEL, N_Q_HEADS * HEAD_DIM
    kvd = N_KV_HEADS * HEAD_DIM

    def nrm(k, shape, scale):
        return jax.random.normal(k, shape, f32) * scale

    return {
        "x": jax.random.normal(ks[0], (BATCH, SEQ, d), f32),
        "attn_wq": nrm(ks[1], (N_ATTN_LAYERS, d, hd), d ** -0.5),
        "attn_wk": nrm(ks[2], (N_ATTN_LAYERS, d, kvd), d ** -0.5),
        "attn_wv": nrm(ks[3], (N_ATTN_LAYERS, d, kvd), d ** -0.5 * BETA),
        "attn_wo": nrm(ks[4], (N_ATTN_LAYERS, hd, d), hd ** -0.5 * BETA),
        "attn_sinks": nrm(ks[5], (N_ATTN_LAYERS, N_Q_HEADS), 0.5),
        "conv_w_in": nrm(ks[6], (N_CONV_LAYERS, d, 2 * d), d ** -0.5),
        "conv_dw": nrm(ks[7], (N_CONV_LAYERS, CONV_WIDTH, d), CONV_WIDTH ** -0.5),
        "conv_norm_g": 1.0 + nrm(ks[8], (N_CONV_LAYERS, d), 0.02),
        "conv_norm_b": nrm(ks[9], (N_CONV_LAYERS, d), 0.02),
        "conv_w_out": nrm(ks[10], (N_CONV_LAYERS, d, d), d ** -0.5 * BETA),
        "ffn_w_up": nrm(ks[11], (DEPTH, d, 2 * D_FF), d ** -0.5),
        "ffn_dw": nrm(ks[12], (DEPTH, FFN_CONV_WIDTH, 2 * D_FF), FFN_CONV_WIDTH ** -0.5),
        "ffn_w_down": nrm(ks[13], (DEPTH, D_FF, d), D_FF ** -0.5 * BETA),
        "norm_g": 1.0 + nrm(ks[14], (DEPTH, 2, d), 0.02),
        "norm_b": nrm(ks[15], (DEPTH, 2, d), 0.02),
    }

def reference(x, attn_wq, attn_wk, attn_wv, attn_wo, attn_sinks,
              conv_w_in, conv_dw, conv_norm_g, conv_norm_b, conv_w_out,
              ffn_w_up, ffn_dw, ffn_w_down, norm_g, norm_b):
    for i in range(DEPTH):
        j = i // N_MIXERS
        if i % N_MIXERS == 0:
            y = sliding_window_sink_attention(x, attn_wq[j], attn_wk[j], attn_wv[j],
                                              attn_wo[j], attn_sinks[j])
        else:
            y = conformer_conv_module(x, conv_w_in[j], conv_dw[j], conv_norm_g[j],
                                      conv_norm_b[j], conv_w_out[j])
        x = layer_norm(ALPHA * x + y, norm_g[i, 0], norm_b[i, 0])
        y = conv_ffn(x, ffn_w_up[i], ffn_dw[i], ffn_w_down[i])
        x = layer_norm(ALPHA * x + y, norm_g[i, 1], norm_b[i, 1])
    return x


_drawn_inputs = setup_inputs


def setup_inputs(seed=0):
    import zlib

    import numpy as np

    out = dict(_drawn_inputs(seed))
    spreads = {}
    factors = {'attn_sinks': 199.414,
     'conv_norm_g': 69.848,
     'conv_norm_b': 67.961,
     'attn_wq': 3.494,
     'attn_wk': 3.481,
     'attn_wv': 2.712,
     'attn_wo': 2.69}
    for name, (base, spread) in spreads.items():
        noise = np.random.default_rng([zlib.crc32(name.encode()), seed]).standard_normal(out[name].shape)
        drawn = base * np.exp(spread * noise) if base else spread * noise
        out[name] = __import__('jax').numpy.asarray(drawn.astype(out[name].dtype))
    for name, factor in factors.items():
        out[name] = (out[name] * factor).astype(out[name].dtype)
    return out
```

```python
from contextlib import ExitStack

import numpy as np

import concourse.bass as bass
from concourse import mybir

ACT = mybir.ActivationFunctionType
ALU = mybir.AluOpType
AX = mybir.AxisListType
F32 = mybir.dt.float32
F32R = mybir.dt.float32r

P = 128
T = 256
TT = T // P
D = 2048
KD = D // P
F = 5632
KF = F // P
HD = 64
NH = D // HD
NKV = 8
GR = NH // NKV
KVD = NKV * HD
CHUNK = 64
ROT = HD // 4
RH = ROT // 2
CW = 31
FW = 3
DEPTH = 2
EPS = 1e-5
ALPHA = (2.0 * DEPTH) ** 0.25
SCALE = HD ** -0.5
BANK = 512
RING = 4
CE = 1024
HALF = D // 2
MASKED = -1e38

TURN = {}
_t = 0
for _name, _elements in (("wk", D * KVD), ("wv", D * KVD), ("wq", D * D), ("wo", D * D), ("up0", D * 2 * F),
                         ("down0", F * D), ("w_in", D * 2 * D), ("w_out", D * D), ("up1", D * 2 * F),
                         ("down1", F * D)):
    TURN[_name] = _t
    _t += _elements // (P * CE * RING)
TURNS = _t


def broadcast_rows(vector, n=P):
    return bass.AP(tensor=vector.tensor, offset=vector.offset, ap=[[0, n]] + [list(d) for d in vector.ap[1:]])


def trunk(nc, x_in, wq, wk, wv, wo, sinks, w_in, conv_dw, conv_g, conv_b, w_out, w_up, ffn_dw, w_down,
          norm_g, norm_b, rope, out):
    with ExitStack() as ctx:
        sem_count = [0]

        def sem(name):
            sem_count[0] += 1
            return ctx.enter_context(nc.semaphore(name))

        ARENA = 212832
        arena = ctx.enter_context(nc.sbuf_tensor("arena", [P, ARENA // 4], F32))

        small_at = [0]
        place = [0]

        def at(name, shape, dt, offset):
            return nc.alloc_sbuf_tensor_at(name, shape, dt, offset=START + offset)


        START = ARENA_START(nc, arena)

        def put(name, shape, dt):
            size = int(np.prod(shape[1:])) * 4
            t = at(name, shape, dt, place[0])
            place[0] += (size + 31) // 32 * 32
            assert place[0] <= ARENA, (name, place[0])
            return t

        x = put("x", [P, TT, D], F32)
        XT_AT = place[0]
        xT = put("xT", [P, KD, 2 * T], F32R)
        HT_AT = place[0]
        hT = put("hT", [P, KF, 2 * T], F32R)
        raw = put("raw", [P, RING, CE], F32)
        w_hi = put("w_hi", [P, RING, CE], F32R)
        w_lo = put("w_lo", [P, RING, CE], F32R)
        ident = put("ident", [P, P], F32)
        norm_cols = put("norm_cols", [P, 2 * 2 * DEPTH, KD], F32)
        conv_cols = put("conv_cols", [P, 2, KD], F32)
        ffn_taps = put("ffn_taps", [P, DEPTH, FW, 2 * KF], F32)
        conv_taps = put("conv_taps", [P, KD, CW], F32)
        stats = put("stats", [P, TT, 4, 6], F32)
        mv = put("mv", [P, TT, 2], F32)
        var_eps = put("var_eps", [P, TT], F32)
        std = put("std", [P, TT], F32)
        rstd = put("rstd", [P, 2, TT], F32)
        newton = put("newton", [P, 3, TT], F32)
        shift = put("shift", [P, TT], F32)
        eps = put("eps", [P, 1], F32)
        turned = put("turned", [P, 2, 2, T], F32)
        cross = put("cross", [P, 2, 2, T], F32)
        up = put("up", [P, 2, 2, T], F32)
        conv = put("conv", [P, 2, 2, T], F32)
        act = put("act", [P, 2, T], F32)

        rows = at("rows", [P, 2, D], F32, XT_AT)
        scores = at("scores", [P, 2, GR, T], F32, XT_AT)
        probs = at("probs", [P, 2, GR, T], F32, XT_AT + 8192)
        probsT = at("probsT", [P, 2, 2 * GR, P], F32, XT_AT + 16384)
        hole = HT_AT + KD * 2 * T * 4
        q_tok = at("q_tok", [P, TT, NKV // 2, GR, 2, HD], F32, hole)
        qT = at("qT", [P, NH // 2, T], F32, hole + 16384)
        k_tok = at("k_tok", [P, TT, KVD], F32, hole + 32768)
        kT = at("kT", [P, NKV // 2, T], F32, hole + 36864)
        v_tok = at("v_tok", [P, TT, KVD], F32, hole + 40960)
        o_at = hole + 45056
        mask = at("mask", [P, P + T], F32, o_at)
        sink = at("sink", [P, NH], F32, o_at + 1536)
        rope_sb = at("rope_sb", [P, TT, 2 * ROT], F32, o_at + 1664)
        rot = at("rot", [P, 2, 8, ROT], F32, o_at + 1920)
        smalls = at("smalls", [P, 2, 8, GR], F32, o_at + 2944)
        conv_out = at("conv_out", [P, KD, T], F32, hole)
        glu = at("glu", [P, 2, CW - 1 + T], F32, hole + 16384)
        silu_out = at("silu_out", [P, 2, T], F32, hole + 16384 + 2304)
        norm_rows = at("norm_rows", [P, P], F32, HT_AT)
        convn_rows = at("convn_rows", [2 * KD, P], F32, HT_AT + 512)
        tap_rows = at("tap_rows", [2 * KF, DEPTH, FW, P], F32, HT_AT + 1024)
        dw_rows = at("dw_rows", [CW, D], F32, HT_AT + 8192)

        ps = ctx.enter_context(nc.psum_tensor("ps", [P, 8, BANK], F32))

        raw_landed = [sem(f"raw_landed{s}") for s in range(RING)]
        hi_ready, lo_ready, chunks_done = sem("hi_ready"), sem("lo_ready"), sem("chunks_done")
        x_landed = [sem(f"x_landed{i}") for i in range(4)]
        vectors_landed, rope_landed, sink_landed = sem("vectors_landed"), sem("rope_landed"), sem("sink_landed")
        ident_made, vectors_turned, vectors_ready = sem("ident_made"), sem("vectors_turned"), sem("vectors_ready")
        x_turned, x_hi, x_lo = sem("x_turned"), sem("x_hi"), sem("x_lo")
        stored = sem("stored")
        rows_landed = [sem(f"rows_landed{i}") for i in range(4)]
        rows_used = sem("rows_used")
        dve_const, mask_made = sem("dve_const"), sem("mask_made")

        w_view = {
            "wk": wk[0].rearrange("(k p) c -> p k c", p=P), "wv": wv[0].rearrange("(k p) c -> p k c", p=P),
            "wq": wq[0].rearrange("(k p) c -> p k c", p=P), "wo": wo[0].rearrange("(k p) c -> p k c", p=P),
            "w_out": w_out[0].rearrange("(k p) c -> p k c", p=P),
            "w_in": w_in[0].rearrange("(k p) (s c) -> p k s c", p=P, s=2),
        }
        for l in range(DEPTH):
            w_view[f"up{l}"] = w_up[l].rearrange("(k p) (s c) -> p k s c", p=P, s=2)
            w_view[f"down{l}"] = w_down[l].rearrange("(k p) c -> p k c", p=P)

        def load(sp, turn, slot, sources):
            if not (isinstance(turn, int) and turn == 0):
                sp.wait_ge(lo_ready, turn * RING + (slot + 1 - RING))
            for i, source in enumerate(sources):
                to = raw[:, slot, i * (CE // 2):(i + 1) * (CE // 2)]
                if len(source.shape) == 3:
                    to = to.rearrange("p (a c) -> p a c", a=2)
                sp.dma_start(to, source).then_inc(raw_landed[slot], 16)

        def round_hi(a, turn, slot):
            a.wait_ge(raw_landed[slot], turn * 32 + 32)
            if not (isinstance(turn, int) and turn == 0):
                a.wait_ge(chunks_done, turn * RING + (slot + 1 - RING))
            nc.scalar.activation(w_hi[:, slot, :], raw[:, slot, :], ACT.Copy).then_inc(hi_ready, 1)

        def take_lo(v, turn, slot):
            v.wait_ge(hi_ready, turn * RING + (slot + 1))
            nc.vector.tensor_tensor(w_lo[:, slot, :], raw[:, slot, :], w_hi[:, slot, :].bitcast(F32),
                                    ALU.subtract).then_inc(lo_ready, 1)

        SPLIT = {}

        def splits(eng, turn, slots=range(RING)):
            for s in slots:
                (round_hi if eng is SPLIT["act"] else take_lo)(eng, turn, s)

        def split_turns(eng, first, n):
            if n == 1:
                splits(eng, first)
            elif n > 1:
                with eng.Fori(0, n) as r:
                    splits(eng, r + first)

        def rows_chunk(pe, turn, slot, src, parts, first, last, bank_free=None, bank_done=None):
            pe.wait_ge(lo_ready, turn * RING + (slot + 1))
            for n, (bank, tok, products) in enumerate(parts):
                if first and bank_free is not None:
                    bank_free(n)
                for j, (k, col) in enumerate(products):
                    hi = src[:, k, tok * P:(tok + 1) * P]
                    lo = src[:, k, T + tok * P:T + (tok + 1) * P]
                    wh = w_hi[:, slot, col:col + BANK]
                    wl = w_lo[:, slot, col:col + BANK]
                    nc.tensor.matmul(ps[:, bank, :], hi, wh, start=(first and j == 0), stop=False)
                    nc.tensor.matmul(ps[:, bank, :], hi, wl, start=False, stop=False)
                    mm = nc.tensor.matmul(ps[:, bank, :], lo, wh, start=False,
                                          stop=(last and j == len(products) - 1))
                if last and n < len(parts) - 1:
                    mm.then_inc(bank_done, 1)
            mm.then_inc(chunks_done, 1)

        def halves(pe, name, src, kt, free, done):
            with pe.Fori(0, 2) as h:
                for k in range(kt):
                    turn = h * (kt // RING) + (TURN[name] + k // RING)
                    parts = [(tok * 2 + n, tok, [(k, n * BANK)]) for tok in range(TT) for n in range(2)]
                    rows_chunk(pe, turn, k % RING, src, parts, k == 0, k == kt - 1,
                               lambda b: pe.wait_ge(free, h * (b + 1) + 1), done)

        def groups(pe, name, n_groups, free):
            with pe.Fori(0, n_groups // 2) as pair:
                for b in range(2):
                    for j in range(KD // 2):
                        slot = j % RING
                        turn = pair * 4 + (TURN[name] + 2 * b + j // RING)
                        if j == 0:
                            pe.wait_ge(free, pair * 4 + (2 * b + 2))
                        pe.wait_ge(lo_ready, turn * RING + (slot + 1))
                        for m in range(4):
                            for kk in range(2):
                                k = 2 * j + kk
                                bank = 4 * b + m
                                col = (m // 2) * 512 + kk * 256 + (m % 2) * P
                                def low():
                                    nc.tensor.matmul(ps[:, bank, 0:T], w_lo[:, slot, col:col + P], xT[:, k, 0:T],
                                                     start=False, stop=False, skip_group_check=True)
                                if k > 0:
                                    low()
                                mm = nc.tensor.matmul(ps[:, bank, :], w_hi[:, slot, col:col + P], xT[:, k, :],
                                                      start=(k == 0), stop=(k == KD - 1), skip_group_check=True)
                                if k == 0:
                                    low()
                        mm.then_inc(chunks_done, 1)

        def group_loads(sp, name, n_groups):
            with sp.Fori(0, n_groups) as g:
                for j in range(KD // 2):
                    v = w_view[name]
                    load(sp, g * 2 + (TURN[name] + j // RING), j % RING,
                         [v[:, 2 * j:2 * j + 2, s, bass.ds(g * 256, 256)] for s in range(2)])

        def half_loads(sp, name, kt):
            with sp.Fori(0, 2) as h:
                for k in range(kt):
                    v = w_view[name]
                    load(sp, h * (kt // RING) + (TURN[name] + k // RING), k % RING,
                         [v[:, k, bass.ds(h * HALF + n * BANK, BANK)] for n in range(2)])

        def half_loads_k(sp, name, kt):
            with sp.Fori(0, 2) as h:
                with sp.Fori(0, kt // RING) as r:
                    for s in range(RING):
                        v = w_down[int(name[-1])]
                        rowsv = v[bass.ds(r * (RING * P) + s * P, P), bass.ds(h * HALF, HALF)]
                        load(sp, h * (kt // RING) + r + TURN[name], s,
                             [rowsv[:, n * BANK:(n + 1) * BANK] for n in range(2)])

        class Norm:
            def __init__(self, n):
                self.n = n
                self.bank_done = sem(f"bank_done{n}")
                self.summed = sem(f"summed{n}")
                self.stats = sem(f"stats{n}")
                self.small = sem(f"small{n}")
                self.std = sem(f"std{n}")
                self.centred = sem(f"centred{n}")
                self.turned = sem(f"turned{n}")
                self.affine = sem(f"affine{n}")
                self.hi = sem(f"xT_hi{n}")
                self.lo = sem(f"xT_lo{n}")
        norms = [Norm(n) for n in range(4)]
        res = sem("residual")

        class Group:
            def __init__(self, n):
                self.free = sem(f"acc_free{n}")
                self.cross = sem(f"cross{n}")
                self.taps = sem(f"taps{n}")
                self.act = sem(f"gate_act{n}")
                self.gated = sem(f"gated{n}")
                self.hi = sem(f"hT_hi{n}")
                self.lo = sem(f"hT_lo{n}")
        ffn = [Group("_up0"), Group("_up1")]
        cin = Group("_in")
        glu_done, pads_made = sem("glu_done"), sem("pads_made")

        NT = 4 * FW

        def ffn_act_1(a, l, g, b, turn0):
            s = ffn[l]
            a.wait_ge(chunks_done, (turn0 + g * 2 + 2) * RING)
            for side in range(2):
                a.wait_ge(s.free, g * 2 + (side + 1 + 2))
                nc.scalar.activation(cross[:, side], ps[:, 4 * b + 2 * side:4 * b + 2 * side + 2, T:2 * T],
                                     ACT.Copy).then_inc(s.cross, 1)

        def ffn_act_2(a, l, g):
            s = ffn[l]
            a.wait_ge(s.taps, (g + 1) * NT + 1)
            a.wait_ge(s.gated, g + 1)
            nc.scalar.activation(act[:], conv[:, 0], ACT.Silu).then_inc(s.act, 1)
            a.wait_ge(s.gated, g + 2)
            nc.scalar.activation(hT[:, bass.ds(g * 2, 2), 0:T], up[:, 0], ACT.Copy).then_inc(s.hi, 1)

        def add_cross(v, s, g, b):
            for side in range(2):
                v.wait_ge(s.cross, g * 2 + (side + 1))
                nc.vector.tensor_tensor(up[:, side], cross[:, side],
                                        ps[:, 4 * b + 2 * side:4 * b + 2 * side + 2, 0:T], ALU.add
                                        ).then_inc(s.free, 1)

        def ffn_dve_1(v, l, g, b):
            s = ffn[l]
            v.wait_ge(s.hi, g + 1)
            v.wait_ge(s.lo, g + 1)
            v.wait_ge(s.taps, g * NT + 1)
            add_cross(v, s, g, b)
            tiles = [(side, m) for side in range(2) for m in range(2)]
            for j in range(FW):
                for n, (side, m) in enumerate(tiles):
                    tap = ffn_taps[:, l, FW - 1 - j, bass.ds(g * 2 + (side * KF + m), 1)]
                    if j == 0:
                        v.wait_ge(s.free, g * 2 + (side + 1 + 4))
                        if n == 0:
                            v.wait_ge(s.act, g + 1)
                            v.wait_ge(s.gated, g + 1)
                        nc.vector.tensor_scalar(conv[:, side, m], up[:, side, m], tap, None, ALU.mult
                                                ).then_inc(s.taps, 1)
                    else:
                        v.wait_ge(s.taps, g * NT + (4 * j - 2 + n))
                        nc.vector.scalar_tensor_tensor(
                            out=conv[:, side, m, j:T], in0=up[:, side, m, 0:T - j], scalar=tap,
                            in1=conv[:, side, m, j:T], op0=ALU.mult, op1=ALU.add).then_inc(s.taps, 1)

        def ffn_dve_2(v, l, g):
            s = ffn[l]
            v.wait_ge(s.act, g + 2)
            v.wait_ge(s.taps, (g + 1) * NT + 1)
            nc.vector.tensor_tensor(up[:, 0], act[:], conv[:, 1], ALU.mult).then_inc(s.gated, 1)
            v.wait_ge(s.gated, g + 2)
            v.wait_ge(s.hi, g + 2)
            h = hT[:, bass.ds(g * 2, 2), :]
            nc.vector.tensor_tensor(h[:, :, T:2 * T], up[:, 0], h[:, :, 0:T].bitcast(F32), ALU.subtract
                                    ).then_inc(s.lo, 1)

        def cin_act(a, g, b, turn0):
            s = cin
            a.wait_ge(chunks_done, (turn0 + g * 2 + 2) * RING)
            for side in range(2):
                a.wait_ge(s.free, g * 2 + (side + 1 + 2))
                nc.scalar.activation(cross[:, side], ps[:, 4 * b + 2 * side:4 * b + 2 * side + 2, T:2 * T],
                                     ACT.Copy).then_inc(s.cross, 1)
            a.wait_ge(s.free, g * 2 + 6)
            a.wait_ge(glu_done, g + 1)
            nc.scalar.activation(act[:], up[:, 1], ACT.Sigmoid).then_inc(s.act, 1)

        def cin_glu(v, g, b):
            s = cin
            v.wait_ge(s.act, g + 1)
            v.wait_ge(glu_done, g + 1)
            add_cross(v, s, g, b)
            v.wait_ge(s.act, g + 2)
            v.wait_ge(s.free, g * 2 + 6)
            v.wait_ge(s.taps, g * (2 * CW) + 1)
            nc.vector.tensor_tensor(glu[:, :, CW - 1:], up[:, 0], act[:], ALU.mult).then_inc(glu_done, 1)

        def cin_tap(v, g, j):
            s = cin
            for m in range(2):
                tap = conv_taps[:, bass.ds(g * 2 + m, 1), j]
                o = conv_out[:, bass.ds(g * 2 + m, 1), :]
                i = glu[:, m:m + 1, j:j + T]
                if j == 0:
                    v.wait_ge(glu_done, g + 2)
                    nc.vector.tensor_scalar(o, i, tap, None, ALU.mult).then_inc(s.taps, 1)
                else:
                    v.wait_ge(s.taps, g * (2 * CW) + (2 * j + m))
                    nc.vector.scalar_tensor_tensor(out=o, in0=i, scalar=tap, in1=o, op0=ALU.mult, op1=ALU.add
                                                   ).then_inc(s.taps, 1)

        def bank_complete(v, s, name, kt, h, b):
            if b < 3:
                v.wait_ge(s.bank_done, 3 * h + b + 1)
            else:
                v.wait_ge(chunks_done, TURN[name] * RING + kt * (h + 1))

        def add_residual(v, n, name, kt, h):
            s = norms[n]
            for b in range(4):
                tok, c = b // 2, h * 2 + b % 2
                cols = x[:, tok, c * BANK:(c + 1) * BANK]
                bank_complete(v, s, name, kt, h, b)
                nc.vector.scalar_tensor_tensor(out=cols, in0=cols, scalar=ALPHA, in1=ps[:, b, :],
                                               op0=ALU.mult, op1=ALU.add).then_inc(s.summed, 1)
                if b > 0:
                    stat(v, s, h, b - 1)
            stat(v, s, h, 3)

        def stat(v, s, h, b):
            tok, c = b // 2, h * 2 + b % 2
            v.wait_ge(s.summed, 4 * h + b + 2)
            nc.vector.bn_stats(stats[:, tok, c, :], x[:, tok, c * BANK:(c + 1) * BANK]).then_inc(s.stats, 1)

        def deviation(v, small, std_sem, stats_sem, n_stats, step=0):
            v.wait_ge(stats_sem, n_stats)
            for tok in range(TT):
                nc.vector.bn_aggr(mv[:, tok, :], stats[:, tok]).then_inc(small, 1)
            v.wait_ge(small, 2)
            nc.vector.tensor_scalar(var_eps[:], mv[:, :, 1], EPS, None, ALU.add).then_inc(small, 1)
            v.wait_ge(std_sem, 1)
            nc.vector.reciprocal(rstd[:, 1], std[:]).then_inc(small, 1)
            v.wait_ge(small, 4)
            nc.vector.tensor_tensor(newton[:, 0], rstd[:, 1], rstd[:, 1], ALU.mult).then_inc(small, 1)
            v.wait_ge(small, 5)
            nc.vector.tensor_tensor(newton[:, 1], newton[:, 0], var_eps[:], ALU.mult).then_inc(small, 1)
            v.wait_ge(small, 6)
            nc.vector.tensor_scalar(newton[:, 2], newton[:, 1], -0.5, 1.5, ALU.mult, ALU.add).then_inc(small, 1)
            v.wait_ge(small, 7)
            nc.vector.tensor_tensor(rstd[:, 0], rstd[:, 1], newton[:, 2], ALU.mult).then_inc(small, 1)
            v.wait_ge(small, 8)

        def root(a, small, std_sem):
            a.wait_ge(small, 3)
            nc.scalar.activation(std[:], var_eps[:], ACT.Sqrt).then_inc(std_sem, 1)

        def centre(v, n):
            s = norms[n]
            for c in range(4):
                for tok in range(TT):
                    cols = x[:, tok, c * BANK:(c + 1) * BANK]
                    nc.vector.tensor_scalar(cols, cols, mv[:, tok, 0:1], rstd[:, 0, tok:tok + 1],
                                            ALU.subtract, ALU.mult).then_inc(s.centred, 1)

        def turn_pe(pe, n):
            s = norms[n]
            for j in range(KD // 2):
                pe.wait_ge(s.centred, 2 * (j // 2 + 1))
                if j >= 4:
                    pe.wait_ge(s.affine, 2 * (j - 3))
                turn_job(pe, 4 + j % 4, j).then_inc(s.turned, 1)

        def turn_job(pe, bank, j):
            for kk in range(2):
                for tok in range(TT):
                    k = 2 * j + kk
                    mm = nc.tensor.transpose(ps[:, bank, kk * T + tok * P:kk * T + (tok + 1) * P],
                                             x[:, tok, k * P:(k + 1) * P], ident[:])
            return mm

        def turn_dve(v, n):
            s = norms[n]

            def affine(j):
                v.wait_ge(s.turned, j + 1)
                if j >= 2:
                    v.wait_ge(s.hi, j - 1)
                    v.wait_ge(s.lo, j - 1)
                for kk in range(2):
                    k = 2 * j + kk
                    nc.vector.tensor_scalar(turned[:, j % 2, kk], ps[:, 4 + j % 4, kk * T:(kk + 1) * T],
                                            norm_cols[:, n, k:k + 1], norm_cols[:, 4 + n, k:k + 1],
                                            ALU.mult, ALU.add).then_inc(s.affine, 1)

            def low(j):
                v.wait_ge(s.hi, j + 1)
                v.wait_ge(s.affine, 2 * j + 2)
                hi = xT[:, 2 * j:2 * j + 2, 0:T].bitcast(F32)
                nc.vector.tensor_tensor(xT[:, 2 * j:2 * j + 2, T:2 * T], turned[:, j % 2], hi,
                                        ALU.subtract).then_inc(s.lo, 1)

            affine(0)
            for j in range(KD // 2):
                if j + 1 < KD // 2:
                    affine(j + 1)
                low(j)

        def turn_act(a, n):
            s = norms[n]
            for j in range(KD // 2):
                a.wait_ge(s.affine, 2 * j + 2)
                nc.scalar.activation(xT[:, 2 * j:2 * j + 2, 0:T], turned[:, j % 2], ACT.Copy).then_inc(s.hi, 1)

        def residual_piece(v, n, c):
            if c == 0:
                v.wait_ge(rows_landed[n], 32)
            for tok in range(TT):
                cols = x[:, tok, c * BANK:(c + 1) * BANK]
                nc.vector.tensor_tensor(cols, cols, rows[:, 0, c * BANK:(c + 1) * BANK], ALU.mult
                                        ).then_inc(res, 1)
            for tok in range(TT):
                cols = x[:, tok, c * BANK:(c + 1) * BANK]
                v.wait_ge(res, n * 16 + 4 * c + tok + 1)
                nc.vector.tensor_tensor(cols, cols, rows[:, 1, c * BANK:(c + 1) * BANK], ALU.add
                                        ).then_inc(res, 1)

        def half_phase(eng, name, kt, after_half, update=None, ahead=True):
            n = kt // RING
            for h in range(2):
                first = TURN[name] + h * n + 1
                more = ahead or h == 0
                if update is not None and h == 0:
                    splits(eng, first)
                    for s in range(RING):
                        update(s)
                        splits(eng, first + 1, [s])
                    split_turns(eng, first + 2, n - 3)
                else:
                    split_turns(eng, first, n - 1)
                if more:
                    splits(eng, first + n - 1, range(RING - 1))
                after_half(h)
                if more:
                    splits(eng, first + n - 1, [RING - 1])

        k_tok_done, rotated, qk_turned, qk_ready = sem("k_tok_done"), sem("rotated"), sem("qk_turned"), sem("qk_ready")
        rot_step, copied, q_done = sem("rot_step"), sem("copied"), sem("q_done")
        sc_done, sc_masked, mx_step, neg_max = sem("sc_done"), sem("sc_masked"), sem("mx_step"), sem("neg_max")
        exp_done, den_step, norm_done = sem("exp_done"), sem("den_step"), sem("norm_done")
        pT_turned, pT_ready, o_done, o_hi, o_lo = (sem("pT_turned"), sem("pT_ready"), sem("o_done"), sem("o_hi"),
                                                   sem("o_lo"))
        UNITS = [(n, t) for n in range(NKV) for t in range(TT)]

        def width(t):
            return (t + 1) * P

        def psum_scores(u):
            t = UNITS[u][1]
            b = 2 * (u % 2)
            v = ps[:, b:b + 1 + t, :]
            return v.rearrange("p b (g k) -> p (b g) k", k=width(t))

        def rotate(v, view, tok, i):
            h = view.shape[1]
            c = rope_sb[:, tok, 0:ROT].unsqueeze(1).broadcast_to([P, h, ROT])
            s = rope_sb[:, tok, ROT:2 * ROT].unsqueeze(1).broadcast_to([P, h, ROT])
            v.wait_ge(copied, i + 1)
            if i >= 1:
                v.wait_ge(rotated, i)
            nc.vector.tensor_tensor(rot[:, 0, 0:h], view[:, :, 0:ROT], c, ALU.mult).then_inc(rot_step, 1)
            nc.vector.tensor_tensor(rot[:, 1, 0:h, 0:RH], view[:, :, RH:ROT], s[:, :, 0:RH], ALU.mult
                                    ).then_inc(rot_step, 1)
            nc.vector.tensor_tensor(rot[:, 1, 0:h, RH:ROT], view[:, :, 0:RH], s[:, :, RH:ROT], ALU.mult
                                    ).then_inc(rot_step, 1)
            v.wait_ge(rot_step, 3 * (i + 1))
            nc.vector.tensor_tensor(view[:, :, 0:ROT], rot[:, 0, 0:h], rot[:, 1, 0:h], ALU.add
                                    ).then_inc(rotated, 1)

        def q_view(tok, i):
            return q_tok[:, tok, i].rearrange("p g e d -> p (g e) d")

        kv_bank_done, q_bank_done, q_free = sem("kv_bank_done"), sem("q_bank_done"), sem("q_free")
        v_copied = sem("v_copied")

        c_turned, c_stats, c_small, c_std, c_shift = (sem("c_turned"), sem("c_stats"), sem("c_small"), sem("c_std"),
                                                      sem("c_shift"))
        c_bcast, c_scaled, c_norm, c_silu, s_hi, s_lo = (sem("c_bcast"), sem("c_scaled"), sem("c_norm"),
                                                         sem("c_silu"), sem("s_hi"), sem("s_lo"))

        block = ctx.enter_context(nc.Block())

        @block.sync
        def _(sp):
            for i in range(4):
                for tok in range(TT):
                    sp.dma_start(x[:, tok, i * BANK:(i + 1) * BANK],
                                 x_in[0, tok * P:(tok + 1) * P, i * BANK:(i + 1) * BANK]
                                 ).then_inc(x_landed[i], 16)
            for name in ("wk", "wv"):
                for j in range(KD // 2):
                    load(sp, TURN[name] + j // RING, j % RING,
                         [w_view[name][:, 2 * j + kk, :] for kk in range(2)])
            half_loads(sp, "wq", KD)
            half_loads(sp, "wo", KD)
            group_loads(sp, "up0", KF // 2)
            half_loads_k(sp, "down0", KF)
            group_loads(sp, "w_in", KD // 2)
            half_loads(sp, "w_out", KD)
            group_loads(sp, "up1", KF // 2)
            half_loads_k(sp, "down1", KF)
            for c in range(4):
                sp.wait_ge(res, 3 * 16 + 4 * (c + 1))
                for tok in range(TT):
                    sp.dma_start(out[0, tok * P:(tok + 1) * P, c * BANK:(c + 1) * BANK],
                                 x[:, tok, c * BANK:(c + 1) * BANK]).then_inc(stored, 16)
            sp.wait_ge(stored, 16 * 4 * TT)

        @block.gpsimd
        def _(pool):
            nc.gpsimd.memset(ident[:], 1.0).then_inc(ident_made, 1)
            pool.wait_ge(ident_made, 1)
            nc.gpsimd.affine_select(out=ident[:], in_=ident[:], compare_op=ALU.is_equal, fill=0.0, base=0,
                                    pattern=[[-1, P]], channel_multiplier=1).then_inc(ident_made, 1)
            for i, v in enumerate((norm_g, norm_b)):
                pool.dma_start(norm_rows[64 * i:64 * (i + 1), :], v.rearrange("l s (t p) -> (l s t) p", p=P)
                               ).then_inc(vectors_landed, 16)
            for i, v in enumerate((conv_g, conv_b)):
                pool.dma_start(convn_rows[KD * i:KD * (i + 1), :], v[0].rearrange("(t p) -> t p", p=P)
                               ).then_inc(vectors_landed, 16)
            for l in range(DEPTH):
                pool.dma_start(tap_rows[:, l], ffn_dw[l].rearrange("j (t p) -> t j p", p=P)
                               ).then_inc(vectors_landed, 16)
            pool.dma_start(dw_rows[:], conv_dw[0]).then_inc(vectors_landed, 16)
            pool.dma_start(rope_sb[:], rope.rearrange("(t p) c -> p t c", p=P)).then_inc(rope_landed, 16)
            pool.dma_start(sink[:], broadcast_rows(sinks)).then_inc(sink_landed, 16)
            for n, name in ((0, "down0"), (1, "w_out"), (2, "down1")):
                pool.wait_ge(chunks_done, TURN[name] * RING)
                for i, v in enumerate((norm_g, norm_b)):
                    pool.dma_start(rows[:, i, :], broadcast_rows(v[n // 2, n % 2:n % 2 + 1])
                                   ).then_inc(rows_landed[n], 16)
            pool.wait_ge(res, 3 * 16)
            for i, v in enumerate((norm_g, norm_b)):
                pool.dma_start(rows[:, i, :], broadcast_rows(v[1, 1:2])).then_inc(rows_landed[3], 16)

        @block.scalar
        def _(a):
            SPLIT["act"] = a
            for s in (ffn[0].act, ffn[0].hi, ffn[1].act, ffn[1].hi, cin.act):
                a.sem_inc(s, 1)
            for j in range(KD // 2):
                a.wait_ge(x_turned, j + 1)
                nc.scalar.activation(xT[:, 2 * j:2 * j + 2, 0:T],
                                     ps[:, j % 4, :].rearrange("p (k t) -> p k t", k=2), ACT.Copy
                                     ).then_inc(x_hi, 1)
                if j < RING:
                    round_hi(a, 0, j)
            for t in range(1, TURN["wq"] + 1):
                if t == TURN["wq"]:
                    splits(a, t, range(RING - 1))
                    for tok in range(TT):
                        if tok == 0:
                            a.wait_ge(kv_bank_done, 2)
                        else:
                            a.wait_ge(chunks_done, TURN["wq"] * RING)
                        nc.scalar.activation(v_tok[:, tok], ps[:, 2 + tok, :], ACT.Copy).then_inc(v_copied, 1)
                    splits(a, t, [RING - 1])
                else:
                    splits(a, t)
                    if t == TURN["wv"]:
                        for tok in range(TT):
                            if tok == 0:
                                a.wait_ge(kv_bank_done, 1)
                            else:
                                a.wait_ge(chunks_done, TURN["wv"] * RING)
                            nc.scalar.activation(k_tok[:, tok], ps[:, tok, :], ACT.Copy).then_inc(copied, 1)

            def q_out(h):
                for b in range(4):
                    tok, i = b // 2, 2 * h + b % 2
                    if b < 3:
                        a.wait_ge(q_bank_done, 3 * h + b + 1)
                    else:
                        a.wait_ge(chunks_done, TURN["wq"] * RING + KD * (h + 1))
                    nc.scalar.activation(q_tok[:, tok, i].rearrange("p g e d -> p e g d"),
                                         ps[:, b, :].rearrange("p (e g d) -> p e g d", e=2, g=GR),
                                         ACT.Copy).then_inc(copied, 1)

            half_phase(a, "wq", KD, q_out)
            for i in range(10):
                a.wait_ge(qk_turned, i + 1)
                if i < 2:
                    to = kT[:, :, i * P:(i + 1) * P]
                else:
                    h, b = (i - 2) // 4, (i - 2) % 4
                    tok, kv = b // 2, 2 * h + b % 2
                    to = qT[:, kv * GR:(kv + 1) * GR, tok * P:(tok + 1) * P]
                nc.scalar.activation(to, ps[:, 4 + i % 4, :].rearrange("p (g t) -> p g t", g=4), ACT.Copy
                                     ).then_inc(qk_ready, 1)

            def exps(u):
                t = UNITS[u][1]
                a.wait_ge(neg_max, u + 1)
                if u >= 2:
                    a.wait_ge(pT_turned, u - 1)
                for g in range(GR):
                    nc.scalar.activation(probs[:, u % 2, g, 0:width(t)], scores[:, u % 2, g, 0:width(t)],
                                         ACT.Exp, bias=smalls[:, u % 2, 2, g:g + 1],
                                         accum_out=smalls[:, u % 2, 4, g:g + 1]).then_inc(exp_done, 1)
                nc.scalar.activation(smalls[:, u % 2, 5], smalls[:, u % 2, 3], ACT.Exp).then_inc(exp_done, 1)

            exps(0)
            for u, (n, t) in enumerate(UNITS):
                if u + 1 < len(UNITS):
                    exps(u + 1)
                a.wait_ge(pT_turned, u + 1)
                if u >= 2:
                    a.wait_ge(o_done, u - 1)
                b = (t + 1) * GR
                nc.scalar.activation(probsT[:, u % 2, 0:b, :],
                                     ps[:, 4:5 + t, :].rearrange("p b (g q) -> p (b g) q", q=P), ACT.Copy
                                     ).then_inc(pT_ready, 1)
                a.wait_ge(o_done, u + 1)
                nc.scalar.activation(hT[:, 2 * n:2 * n + 2, t * P:(t + 1) * P],
                                     ps[:, 6 + u % 2, 0:2 * P].rearrange("p (j q) -> p j q", j=2), ACT.Copy
                                     ).then_inc(o_hi, 1)

            def norm_act(n):
                def after(h):
                    if h == 1:
                        root(a, norms[n].small, norms[n].std)
                        turn_act(a, n)
                return after

            half_phase(a, "wo", KD, norm_act(0))

            def ffn_phase(l):
                t0 = TURN[f"up{l}"]
                with a.Fori(0, KF // 4) as pair:
                    for b in range(2):
                        g = pair * 2 + b
                        splits(a, g * 2 + (t0 + 1))
                        splits(a, g * 2 + (t0 + 2), range(RING - 1))
                        ffn_act_1(a, l, g, b, t0)
                        splits(a, g * 2 + (t0 + 2), [RING - 1])
                        ffn_act_2(a, l, g)

            ffn_phase(0)
            half_phase(a, "down0", KF, norm_act(1))
            t0 = TURN["w_in"]
            with a.Fori(0, KD // 4) as pair:
                for b in range(2):
                    g = pair * 2 + b
                    splits(a, g * 2 + (t0 + 1))
                    splits(a, g * 2 + (t0 + 2), range(RING - 1))
                    cin_act(a, g, b, t0)
                    splits(a, g * 2 + (t0 + 2), [RING - 1])
            root(a, c_small, c_std)
            for j in range(KD // 2):
                a.wait_ge(c_norm, j + 1)
                for kk in range(2):
                    k = 2 * j + kk
                    if j >= 1:
                        a.wait_ge(s_lo, j)
                    nc.scalar.activation(silu_out[:, kk], conv_out[:, k], ACT.Silu, bias=conv_cols[:, 1, k:k + 1],
                                         scale=conv_cols[:, 0, k:k + 1]).then_inc(c_silu, 1)
                a.wait_ge(c_silu, 2 * j + 2)
                nc.scalar.activation(hT[:, 2 * j:2 * j + 2, 0:T], silu_out[:], ACT.Copy).then_inc(s_hi, 1)
            half_phase(a, "w_out", KD, norm_act(2))
            ffn_phase(1)

            def last(h):
                if h == 1:
                    root(a, norms[3].small, norms[3].std)
            half_phase(a, "down1", KF, last, ahead=False)

        @block.vector
        def _(v):
            for s in (ffn[0].taps, ffn[0].gated, ffn[0].lo, ffn[1].taps, ffn[1].gated, ffn[1].lo, cin.taps,
                      glu_done, norms[0].summed, norms[1].summed, norms[2].summed, norms[3].summed):
                v.sem_inc(s, 1)
            nc.vector.memset(mask[:], MASKED).then_inc(mask_made, 1)
            v.wait_ge(mask_made, 1)
            for part, lo, hi in ((0, 0, CHUNK), (64, 0, P), (0, P + CHUNK, P + 3 * CHUNK), (64, 2 * P, 2 * P + P)):
                nc.vector.memset(mask[part:part + CHUNK, lo:hi], 0.0).then_inc(mask_made, 1)
            for j in range(KD // 2):
                v.wait_ge(x_hi, j + 1)
                nc.vector.tensor_tensor(xT[:, 2 * j:2 * j + 2, T:2 * T],
                                        ps[:, j % 4, :].rearrange("p (k t) -> p k t", k=2),
                                        xT[:, 2 * j:2 * j + 2, 0:T].bitcast(F32), ALU.subtract).then_inc(x_lo, 1)
                if j < RING:
                    take_lo(v, 0, j)
            v.wait_ge(vectors_turned, 4)
            nc.vector.tensor_copy(norm_cols[:].rearrange("p a t -> p (a t)"), ps[:, 4, 0:P]).then_inc(vectors_ready, 1)
            nc.vector.tensor_copy(conv_cols[:].rearrange("p a t -> p (a t)"), ps[:, 4, P:P + 2 * KD]
                                  ).then_inc(vectors_ready, 1)
            for l in range(DEPTH):
                nc.vector.tensor_copy(ffn_taps[:, l].rearrange("p j t -> p (j t)"), ps[:, 5 + l, 0:FW * 2 * KF]
                                      ).then_inc(vectors_ready, 1)
            nc.vector.tensor_copy(conv_taps[:].rearrange("p t j -> p (t j)"), ps[:, 7, 0:KD * CW]
                                  ).then_inc(vectors_ready, 1)
            split_turns_from = 1
            for t in range(1, TURN["wq"] + 1):
                splits(v, t, range(RING - 1))
                if t == TURN["wv"] + 1:
                    v.wait_ge(rope_landed, 16)
                    for tok in range(TT):
                        rotate(v, k_tok[:, tok].rearrange("p (h d) -> p h d", d=HD), tok, tok)
                splits(v, t, [RING - 1])

            def q_rot(h):
                for b in range(4):
                    tok, i = b // 2, 2 * h + b % 2
                    rotate(v, q_view(tok, i), tok, 2 + 4 * h + b)

            half_phase(v, "wq", KD, q_rot)

            def masked(u):
                n, t = UNITS[u]
                w = width(t)
                sm = smalls[:, u % 2]
                v.wait_ge(sc_done, u + 1)
                if u >= 2:
                    v.wait_ge(exp_done, 5 * (u - 1))
                    v.wait_ge(neg_max, u - 1)
                m = mask[:, t * P:t * P + w].unsqueeze(1).broadcast_to([P, GR, w])
                nc.vector.scalar_tensor_tensor(out=scores[:, u % 2, :, 0:w], in0=psum_scores(u), scalar=SCALE,
                                               in1=m, op0=ALU.mult, op1=ALU.add).then_inc(sc_masked, 1)
                v.wait_ge(sc_masked, u + 1)
                nc.vector.tensor_reduce(sm[:, 0], scores[:, u % 2, :, 0:w], AX.X, ALU.max).then_inc(mx_step, 1)
                v.wait_ge(mx_step, 3 * u + 1)
                nc.vector.tensor_tensor(sm[:, 1], sm[:, 0], sink[:, n * GR:(n + 1) * GR], ALU.max
                                        ).then_inc(mx_step, 1)
                v.wait_ge(mx_step, 3 * u + 2)
                nc.vector.tensor_tensor(sm[:, 3], sink[:, n * GR:(n + 1) * GR], sm[:, 1], ALU.subtract
                                        ).then_inc(mx_step, 1)
                v.wait_ge(mx_step, 3 * u + 3)
                nc.vector.tensor_scalar(sm[:, 2], sm[:, 1], -1.0, None, ALU.mult).then_inc(neg_max, 1)

            def normalise(u):
                n, t = UNITS[u]
                sm = smalls[:, u % 2]
                v.wait_ge(exp_done, 5 * (u + 1))
                nc.vector.tensor_tensor(sm[:, 6], sm[:, 4], sm[:, 5], ALU.add).then_inc(den_step, 1)
                v.wait_ge(den_step, 2 * u + 1)
                if u >= 2:
                    v.wait_ge(norm_done, GR * (u - 1))
                nc.vector.reciprocal(sm[:, 7], sm[:, 6]).then_inc(den_step, 1)
                v.wait_ge(den_step, 2 * u + 2)
                for g in range(GR):
                    p = probs[:, u % 2, g, 0:width(t)]
                    nc.vector.tensor_scalar(p, p, sm[:, 7, g:g + 1], None, ALU.mult).then_inc(norm_done, 1)

            v.wait_ge(sink_landed, 16)
            v.wait_ge(mask_made, 5)
            masked(0)
            for u, (n, t) in enumerate(UNITS):
                if u + 1 < len(UNITS):
                    masked(u + 1)
                normalise(u)
                v.wait_ge(o_hi, u + 1)
                nc.vector.tensor_tensor(hT[:, 2 * n:2 * n + 2, T + t * P:T + (t + 1) * P],
                                        ps[:, 6 + u % 2, 0:2 * P].rearrange("p (j q) -> p j q", j=2),
                                        hT[:, 2 * n:2 * n + 2, t * P:(t + 1) * P].bitcast(F32), ALU.subtract
                                        ).then_inc(o_lo, 1)

            def norm_dve(n, name, kt):
                def after(h):
                    add_residual(v, n, name, kt, h)
                    if h == 1:
                        s = norms[n]
                        deviation(v, s.small, s.std, s.stats, 8)
                        centre(v, n)
                        if n < 3:
                            turn_dve(v, n)
                return after

            def banks_free(s, centred, lo):
                v.sem_inc(s.free, 4)

            half_phase(v, "wo", KD, norm_dve(0, "wo", KD))
            banks_free(ffn[0], None, None)

            def ffn_phase(l):
                t0 = TURN[f"up{l}"]
                with v.Fori(0, KF // 4) as pair:
                    for b in range(2):
                        g = pair * 2 + b
                        splits(v, g * 2 + (t0 + 1))
                        splits(v, g * 2 + (t0 + 2), range(RING - 1))
                        ffn_dve_1(v, l, g, b)
                        splits(v, g * 2 + (t0 + 2), [RING - 1])
                        ffn_dve_2(v, l, g)

            ffn_phase(0)
            half_phase(v, "down0", KF, norm_dve(1, "down0", KF), update=lambda c: residual_piece(v, 0, c))
            banks_free(cin, None, None)
            nc.vector.memset(glu[:, :, 0:CW - 1], 0.0).then_inc(pads_made, 1)
            v.wait_ge(pads_made, 1)
            t0 = TURN["w_in"]
            with v.Fori(0, KD // 4) as pair:
                for b in range(2):
                    g = pair * 2 + b
                    splits(v, g * 2 + (t0 + 1))
                    splits(v, g * 2 + (t0 + 2), range(RING - 1))
                    cin_glu(v, g, b)
                    for j in range(CW):
                        cin_tap(v, g, j)
                        if j == 6:
                            splits(v, g * 2 + (t0 + 2), [RING - 1])
            for i in range(8):
                tok, c = i // 4, i % 4
                v.wait_ge(c_turned, i + 1)
                nc.vector.bn_stats(stats[:, tok, c, :], ps[:, i, :]).then_inc(c_stats, 1)
            deviation(v, c_small, c_std, c_stats, 8)
            nc.vector.tensor_tensor(newton[:, 0], mv[:, :, 0], rstd[:, 0], ALU.mult).then_inc(c_small, 1)
            v.wait_ge(c_small, 9)
            nc.vector.tensor_scalar(shift[:], newton[:, 0], -1.0, None, ALU.mult).then_inc(c_shift, 1)
            v.wait_ge(c_bcast, 1)

            def c_step(j):
                o = conv_out[:, 2 * j:2 * j + 2]
                nc.vector.tensor_tensor(o, o, ps[:, 0, 0:T].unsqueeze(1).broadcast_to([P, 2, T]), ALU.mult
                                        ).then_inc(c_scaled, 1)
                v.wait_ge(c_scaled, j + 1)
                nc.vector.tensor_tensor(o, o, ps[:, 0, T:2 * T].unsqueeze(1).broadcast_to([P, 2, T]), ALU.add
                                        ).then_inc(c_norm, 1)
            c_step(0)
            for j in range(KD // 2):
                if j + 1 < KD // 2:
                    c_step(j + 1)
                v.wait_ge(s_hi, j + 1)
                nc.vector.tensor_tensor(hT[:, 2 * j:2 * j + 2, T:2 * T], silu_out[:],
                                        hT[:, 2 * j:2 * j + 2, 0:T].bitcast(F32), ALU.subtract).then_inc(s_lo, 1)
            half_phase(v, "w_out", KD, norm_dve(2, "w_out", KD), update=lambda c: residual_piece(v, 1, c))
            banks_free(ffn[1], None, None)
            ffn_phase(1)
            half_phase(v, "down1", KF, norm_dve(3, "down1", KF), update=lambda c: residual_piece(v, 2, c),
                       ahead=False)
            v.wait_ge(norms[3].centred, 8)
            for c in range(4):
                residual_piece(v, 3, c)

        @block.tensor
        def _(pe):
            pe.wait_ge(ident_made, 2)
            for j in range(KD // 2):
                if j % 2 == 0:
                    pe.wait_ge(x_landed[j // 2], 32)
                if j >= 4:
                    pe.wait_ge(x_lo, j - 3)
                turn_job(pe, j % 4, j).then_inc(x_turned, 1)
            pe.wait_ge(vectors_landed, 16 * 7)
            nc.tensor.transpose(ps[:, 4, 0:P], norm_rows[:], ident[:])
            nc.tensor.transpose(ps[:, 4, P:P + 2 * KD], convn_rows[:], ident[0:2 * KD, 0:2 * KD]
                                ).then_inc(vectors_turned, 1)
            for l in range(DEPTH):
                for j in range(FW):
                    mm = nc.tensor.transpose(ps[:, 5 + l, j * 2 * KF:(j + 1) * 2 * KF], tap_rows[:, l, j, :],
                                             ident[0:2 * KF, 0:2 * KF])
                mm.then_inc(vectors_turned, 1)
            for t in range(KD):
                mm = nc.tensor.transpose(ps[:, 7, t * CW:(t + 1) * CW], dw_rows[:, t * P:(t + 1) * P],
                                         ident[0:CW, 0:CW])
            mm.then_inc(vectors_turned, 1)
            pe.wait_ge(x_lo, KD // 2)
            for i, name in enumerate(("wk", "wv")):
                for j in range(KD // 2):
                    parts = [(2 * i + tok, tok, [(2 * j, 0), (2 * j + 1, BANK)]) for tok in range(TT)]
                    rows_chunk(pe, TURN[name] + j // RING, j % RING, xT, parts, j == 0, j == KD // 2 - 1,
                               None, kv_bank_done)
            pe.wait_ge(copied, 2)
            pe.wait_ge(v_copied, 2)
            with pe.Fori(0, 2) as h:
                for k in range(KD):
                    turn = h * (KD // RING) + (TURN["wq"] + k // RING)
                    parts = [(tok * 2 + n, tok, [(k, n * BANK)]) for tok in range(TT) for n in range(2)]
                    rows_chunk(pe, turn, k % RING, xT, parts, k == 0, k == KD - 1,
                               lambda b: pe.wait_ge(copied, h * (b + 1) + 2), q_bank_done)
            pe.wait_ge(vectors_ready, 5)
            for i in range(10):
                if i >= 4:
                    pe.wait_ge(qk_ready, i - 3)
                pe.wait_ge(rotated, i + 1)
                for j in range(4):
                    if i < 2:
                        src = k_tok[:, i, j * P:(j + 1) * P]
                    else:
                        h, b = (i - 2) // 4, (i - 2) % 4
                        tok, kv = b // 2, 2 * h + b % 2
                        src = q_tok[:, tok, kv, j].rearrange("p e d -> p (e d)")
                    mm = nc.tensor.transpose(ps[:, 4 + i % 4, j * P:(j + 1) * P], src, ident[:])
                mm.then_inc(qk_turned, 1)
            pe.wait_ge(qk_ready, 10)

            def score(u):
                n, t = UNITS[u]
                e, i = n % 2, n // 2
                if u >= 2:
                    pe.wait_ge(sc_masked, u - 1)
                w = width(t)
                o = psum_scores(u)
                for g in range(GR):
                    mm = nc.tensor.matmul(o[:, g, :], qT[64 * e:64 * e + 64, i * GR + g, t * P:(t + 1) * P],
                                          kT[64 * e:64 * e + 64, i, 0:w], start=True, stop=True)
                mm.then_inc(sc_done, 1)

            score(0)
            score(1)
            for u, (n, t) in enumerate(UNITS):
                pe.wait_ge(norm_done, GR * (u + 1))
                if u >= 1:
                    pe.wait_ge(pT_ready, u)
                pt = ps[:, 4:5 + t, :].rearrange("p b (g q) -> p (b g) q", q=P)
                for g in range(GR):
                    for kb in range(t + 1):
                        mm = nc.tensor.transpose(pt[:, g * (t + 1) + kb, :], probs[:, u % 2, g, kb * P:(kb + 1) * P],
                                                 ident[:])
                mm.then_inc(pT_turned, 1)
                if u + 2 < len(UNITS):
                    score(u + 2)
                pe.wait_ge(pT_ready, u + 1)
                if u >= 2:
                    pe.wait_ge(o_lo, u - 1)
                for g in range(GR):
                    r = 64 * (g % 2)
                    o = ps[r:r + 64, 6 + u % 2, (g // 2) * P:(g // 2 + 1) * P]
                    for kb in range(t + 1):
                        mm = nc.tensor.matmul(o, v_tok[:, kb, n * HD:(n + 1) * HD],
                                              probsT[:, u % 2, g * (t + 1) + kb, :], start=(kb == 0), stop=(kb == t))
                mm.then_inc(o_done, 1)
            pe.wait_ge(o_lo, len(UNITS))
            halves(pe, "wo", hT, KD, norms[0].summed, norms[0].bank_done)
            turn_pe(pe, 0)
            pe.wait_ge(norms[0].lo, KD // 2)
            groups(pe, "up0", KF // 2, ffn[0].free)
            pe.wait_ge(ffn[0].lo, KF // 2 + 1)
            halves(pe, "down0", hT, KF, norms[1].summed, norms[1].bank_done)
            turn_pe(pe, 1)
            pe.wait_ge(norms[1].lo, KD // 2)
            groups(pe, "w_in", KD // 2, cin.free)
            for i in range(8):
                tok, c = i // 4, i % 4
                if i < 4:
                    pe.wait_ge(cin.taps, (2 * c + 2) * 2 * CW + 1)
                if i == 0:
                    pe.wait_ge(cin.free, 4 + KD)
                for j in range(4):
                    mm = nc.tensor.transpose(ps[:, i, j * P:(j + 1) * P],
                                             conv_out[:, 4 * c + j, tok * P:(tok + 1) * P], ident[:])
                mm.then_inc(c_turned, 1)
            pe.wait_ge(c_shift, 1)
            for i, col in enumerate((rstd[:, 0], shift[:])):
                for tok in range(TT):
                    mm = nc.tensor.matmul(ps[:, 0, i * T + tok * P:i * T + (tok + 1) * P],
                                          col[:, tok:tok + 1].broadcast_to([P, P]), ident[:], start=True, stop=True)
            mm.then_inc(c_bcast, 1)
            pe.wait_ge(c_norm, KD // 2)
            pe.wait_ge(s_lo, KD // 2)
            halves(pe, "w_out", hT, KD, norms[2].summed, norms[2].bank_done)
            turn_pe(pe, 2)
            pe.wait_ge(norms[2].lo, KD // 2)
            groups(pe, "up1", KF // 2, ffn[1].free)
            pe.wait_ge(ffn[1].lo, KF // 2 + 1)
            halves(pe, "down1", hT, KF, norms[3].summed, norms[3].bank_done)


def ARENA_START(nc, arena):
    return 16512


_INS = ["x", "attn_wq", "attn_wk", "attn_wv", "attn_wo", "attn_sinks", "conv_w_in", "conv_dw", "conv_norm_g",
        "conv_norm_b", "conv_w_out", "ffn_w_up", "ffn_dw", "ffn_w_down", "norm_g", "norm_b"]


def rope_table():
    inv = np.float32(500000.0) ** (-np.arange(0, ROT, 2, dtype=np.float32) / np.float32(ROT))
    ang = np.arange(T, dtype=np.float32)[:, None] * inv.astype(np.float32)[None, :]
    c, s = np.cos(ang).astype(np.float32), np.sin(ang).astype(np.float32)
    return np.ascontiguousarray(np.concatenate([c, c, -s, s], axis=1))


def kernel(**inputs):
    import numpy as _np
    import concourse.bacc as _bacc
    from concourse import mybir as _mybir
    from concourse.bass_utils import run_bass_kernel_spmd as _run

    nc = _bacc.Bacc("TRN2", target_bir_lowering=False, num_devices=1)
    arrays, args = {}, []
    for name in _INS:
        a = _np.ascontiguousarray(inputs[name])
        arrays[f"in_{name}_dram"] = a
        args.append(nc.dram_tensor(f"in_{name}_dram", a.shape, _mybir.dt.from_np(a.dtype), kind="ExternalInput").ap())
    table = rope_table()
    arrays["rope_dram"] = table
    args.append(nc.dram_tensor("rope_dram", table.shape, _mybir.dt.from_np(table.dtype), kind="ExternalInput").ap())
    args.append(nc.dram_tensor("out_dram", (1, T, D), _mybir.dt.from_np(_np.dtype("float32")),
                               kind="ExternalOutput").ap())
    trunk(nc, *args)
    r = _run(nc, [arrays], core_ids=[0])
    return r.results[0]["out_dram"]
```

```python
from contextlib import ExitStack

import numpy as np

import concourse.bass as bass
from concourse import mybir

ACT = mybir.ActivationFunctionType
ALU = mybir.AluOpType
AX = mybir.AxisListType
F32 = mybir.dt.float32
F32R = mybir.dt.float32r

P = 128
T = 256
TT = T // P
D = 2048
KD = D // P
F = 5632
KF = F // P
HD = 64
NH = D // HD
NKV = 8
GR = NH // NKV
KVD = NKV * HD
CHUNK = 64
ROT = HD // 4
RH = ROT // 2
CW = 31
FW = 3
DEPTH = 2
EPS = 1e-5
ALPHA = (2.0 * DEPTH) ** 0.25
SCALE = HD ** -0.5
BANK = 512
RING = 4
CE = 1024
HALF = D // 2
MASKED = -1e38

TURN = {}
_t = 0
for _name, _elements in (("wk", D * KVD), ("wv", D * KVD), ("wq", D * D), ("wo", D * D), ("up0", D * 2 * F),
                         ("down0", F * D), ("w_in", D * 2 * D), ("w_out", D * D), ("up1", D * 2 * F),
                         ("down1", F * D)):
    TURN[_name] = _t
    _t += _elements // (P * CE * RING)
TURNS = _t


def broadcast_rows(vector, n=P):
    return bass.AP(tensor=vector.tensor, offset=vector.offset, ap=[[0, n]] + [list(d) for d in vector.ap[1:]])


def trunk(nc, x_in, wq, wk, wv, wo, sinks, w_in, conv_dw, conv_g, conv_b, w_out, w_up, ffn_dw, w_down,
          norm_g, norm_b, rope, out):
    with ExitStack() as ctx:
        sem_count = [0]

        def sem(name):
            sem_count[0] += 1
            return ctx.enter_context(nc.semaphore(name))

        ARENA = 212832
        arena = ctx.enter_context(nc.sbuf_tensor("arena", [P, ARENA // 4], F32))

        small_at = [0]
        place = [0]

        def at(name, shape, dt, offset):
            return nc.alloc_sbuf_tensor_at(name, shape, dt, offset=START + offset)


        START = ARENA_START(nc, arena)

        def put(name, shape, dt):
            size = int(np.prod(shape[1:])) * 4
            t = at(name, shape, dt, place[0])
            place[0] += (size + 31) // 32 * 32
            assert place[0] <= ARENA, (name, place[0])
            return t

        x = put("x", [P, TT, D], F32)
        XT_AT = place[0]
        xT = put("xT", [P, KD, 2 * T], F32R)
        HT_AT = place[0]
        hT = put("hT", [P, KF, 2 * T], F32R)
        raw = put("raw", [P, RING, CE], F32)
        w_hi = put("w_hi", [P, RING, CE], F32R)
        w_lo = put("w_lo", [P, RING, CE], F32R)
        ident = put("ident", [P, P], F32)
        norm_cols = put("norm_cols", [P, 2 * 2 * DEPTH, KD], F32)
        conv_cols = put("conv_cols", [P, 2, KD], F32)
        ffn_taps = put("ffn_taps", [P, DEPTH, FW, 2 * KF], F32)
        conv_taps = put("conv_taps", [P, KD, CW], F32)
        stats = put("stats", [P, TT, 4, 6], F32)
        mv = put("mv", [P, TT, 2], F32)
        var_eps = put("var_eps", [P, TT], F32)
        std = put("std", [P, TT], F32)
        rstd = put("rstd", [P, 2, TT], F32)
        newton = put("newton", [P, 3, TT], F32)
        shift = put("shift", [P, TT], F32)
        eps = put("eps", [P, 1], F32)
        turned = put("turned", [P, 2, 2, T], F32)
        cross = put("cross", [P, 2, 2, T], F32)
        up = put("up", [P, 2, 2, T], F32)
        conv = put("conv", [P, 2, 2, T], F32)
        act = put("act", [P, 2, T], F32)

        rows = at("rows", [P, 2, D], F32, XT_AT)
        scores = at("scores", [P, 2, GR, T], F32, XT_AT)
        probs = at("probs", [P, 2, GR, T], F32, XT_AT + 8192)
        probsT = at("probsT", [P, 2, 2 * GR, P], F32, XT_AT + 16384)
        hole = HT_AT + KD * 2 * T * 4
        q_tok = at("q_tok", [P, TT, NKV // 2, GR, 2, HD], F32, hole)
        qT = at("qT", [P, NH // 2, T], F32, hole + 16384)
        k_tok = at("k_tok", [P, TT, KVD], F32, hole + 32768)
        kT = at("kT", [P, NKV // 2, T], F32, hole + 36864)
        v_tok = at("v_tok", [P, TT, KVD], F32, hole + 40960)
        o_at = hole + 45056
        mask = at("mask", [P, P + T], F32, o_at)
        sink = at("sink", [P, NH], F32, o_at + 1536)
        rope_sb = at("rope_sb", [P, TT, 2 * ROT], F32, o_at + 1664)
        rot = at("rot", [P, 2, 8, ROT], F32, o_at + 1920)
        smalls = at("smalls", [P, 2, 8, GR], F32, o_at + 2944)
        conv_out = at("conv_out", [P, KD, T], F32, hole)
        glu = at("glu", [P, 2, CW - 1 + T], F32, hole + 16384)
        silu_out = at("silu_out", [P, 2, T], F32, hole + 16384 + 2304)
        norm_rows = at("norm_rows", [P, P], F32, HT_AT)
        convn_rows = at("convn_rows", [2 * KD, P], F32, HT_AT + 512)
        tap_rows = at("tap_rows", [2 * KF, DEPTH, FW, P], F32, HT_AT + 1024)
        dw_rows = at("dw_rows", [CW, D], F32, HT_AT + 8192)

        ps = ctx.enter_context(nc.psum_tensor("ps", [P, 8, BANK], F32))

        raw_landed = [sem(f"raw_landed{s}") for s in range(RING)]
        hi_ready, lo_ready, chunks_done = sem("hi_ready"), sem("lo_ready"), sem("chunks_done")
        x_landed = [sem(f"x_landed{i}") for i in range(4)]
        vectors_landed, rope_landed, sink_landed = sem("vectors_landed"), sem("rope_landed"), sem("sink_landed")
        ident_made, vectors_turned, vectors_ready = sem("ident_made"), sem("vectors_turned"), sem("vectors_ready")
        x_turned, x_hi, x_lo = sem("x_turned"), sem("x_hi"), sem("x_lo")
        stored = sem("stored")
        rows_landed = [sem(f"rows_landed{i}") for i in range(4)]
        rows_used = sem("rows_used")
        dve_const, mask_made = sem("dve_const"), sem("mask_made")

        w_view = {
            "wk": wk[0].rearrange("(k p) c -> p k c", p=P), "wv": wv[0].rearrange("(k p) c -> p k c", p=P),
            "wq": wq[0].rearrange("(k p) c -> p k c", p=P), "wo": wo[0].rearrange("(k p) c -> p k c", p=P),
            "w_out": w_out[0].rearrange("(k p) c -> p k c", p=P),
            "w_in": w_in[0].rearrange("(k p) (s c) -> p k s c", p=P, s=2),
        }
        for l in range(DEPTH):
            w_view[f"up{l}"] = w_up[l].rearrange("(k p) (s c) -> p k s c", p=P, s=2)
            w_view[f"down{l}"] = w_down[l].rearrange("(k p) c -> p k c", p=P)

        def load(sp, turn, slot, sources):
            if not (isinstance(turn, int) and turn == 0):
                sp.wait_ge(lo_ready, turn * RING + (slot + 1 - RING))
            for i, source in enumerate(sources):
                to = raw[:, slot, i * (CE // 2):(i + 1) * (CE // 2)]
                if len(source.shape) == 3:
                    to = to.rearrange("p (a c) -> p a c", a=2)
                sp.dma_start(to, source).then_inc(raw_landed[slot], 16)

        def round_hi(a, turn, slot):
            a.wait_ge(raw_landed[slot], turn * 32 + 32)
            if not (isinstance(turn, int) and turn == 0):
                a.wait_ge(chunks_done, turn * RING + (slot + 1 - RING))
            nc.scalar.activation(w_hi[:, slot, :], raw[:, slot, :], ACT.Copy).then_inc(hi_ready, 1)

        def take_lo(v, turn, slot):
            v.wait_ge(hi_ready, turn * RING + (slot + 1))
            v.tensor_tensor(w_lo[:, slot, :], raw[:, slot, :], w_hi[:, slot, :].bitcast(F32),
                                    ALU.subtract).then_inc(lo_ready, 1)

        SPLIT = {}

        def splits(eng, turn, slots=range(RING)):
            for s in slots:
                (round_hi if eng is SPLIT["act"] else take_lo)(eng, turn, s)

        def split_turns(eng, first, n):
            if n == 1:
                splits(eng, first)
            elif n > 1:
                with eng.Fori(0, n) as r:
                    splits(eng, r + first)

        def rows_chunk(pe, turn, slot, src, parts, first, last, bank_free=None, bank_done=None):
            pe.wait_ge(lo_ready, turn * RING + (slot + 1))
            for n, (bank, tok, products) in enumerate(parts):
                if first and bank_free is not None:
                    bank_free(n)
                for j, (k, col) in enumerate(products):
                    hi = src[:, k, tok * P:(tok + 1) * P]
                    lo = src[:, k, T + tok * P:T + (tok + 1) * P]
                    wh = w_hi[:, slot, col:col + BANK]
                    wl = w_lo[:, slot, col:col + BANK]
                    nc.tensor.matmul(ps[:, bank, :], hi, wh, start=(first and j == 0), stop=False)
                    nc.tensor.matmul(ps[:, bank, :], hi, wl, start=False, stop=False)
                    mm = nc.tensor.matmul(ps[:, bank, :], lo, wh, start=False,
                                          stop=(last and j == len(products) - 1))
                if last and n < len(parts) - 1:
                    mm.then_inc(bank_done, 1)
            mm.then_inc(chunks_done, 1)

        def halves(pe, name, src, kt, free, done, src_ready=None):
            with pe.Fori(0, 2) as h:
                for k in range(kt):
                    turn = h * (kt // RING) + (TURN[name] + k // RING)
                    parts = [(tok * 2 + n, tok, [(k, n * BANK)]) for tok in range(TT) for n in range(2)]
                    if src_ready is not None and k % 2 == 0:
                        pe.wait_ge(src_ready[0], k // 2 + 1 + src_ready[1])
                    rows_chunk(pe, turn, k % RING, src, parts, k == 0, k == kt - 1,
                               lambda b: pe.wait_ge(free, h * (b + 1) + 1), done)

        def groups(pe, name, n_groups, free, before):
            def group(pair, b, before=None):
                for j in range(KD // 2):
                    slot = j % RING
                    turn = pair * 4 + (TURN[name] + 2 * b + j // RING)
                    if j == 0:
                        pe.wait_ge(free, pair * 4 + (2 * b + 2))
                    if before is not None:
                        before(j)
                    pe.wait_ge(lo_ready, turn * RING + (slot + 1))
                    for m in range(4):
                        for kk in range(2):
                            k = 2 * j + kk
                            bank = 4 * b + m
                            col = (m // 2) * 512 + kk * 256 + (m % 2) * P

                            def low():
                                nc.tensor.matmul(ps[:, bank, 0:T], w_lo[:, slot, col:col + P], xT[:, k, 0:T],
                                                 start=False, stop=False, skip_group_check=True)
                            if k > 0:
                                low()
                            mm = nc.tensor.matmul(ps[:, bank, :], w_hi[:, slot, col:col + P], xT[:, k, :],
                                                  start=(k == 0), stop=(k == KD - 1), skip_group_check=True)
                            if k == 0:
                                low()
                    mm.then_inc(chunks_done, 1)
            group(0, 0, before)
            group(0, 1)
            with pe.Fori(1, n_groups // 2) as pair:
                for b in range(2):
                    group(pair, b)

        def group_loads(sp, name, n_groups):
            with sp.Fori(0, n_groups) as g:
                for j in range(KD // 2):
                    v = w_view[name]
                    load(sp, g * 2 + (TURN[name] + j // RING), j % RING,
                         [v[:, 2 * j:2 * j + 2, s, bass.ds(g * 256, 256)] for s in range(2)])

        def half_loads(sp, name, kt):
            with sp.Fori(0, 2) as h:
                for k in range(kt):
                    v = w_view[name]
                    load(sp, h * (kt // RING) + (TURN[name] + k // RING), k % RING,
                         [v[:, k, bass.ds(h * HALF + n * BANK, BANK)] for n in range(2)])

        def half_loads_k(sp, name, kt):
            with sp.Fori(0, 2) as h:
                with sp.Fori(0, kt // RING) as r:
                    for s in range(RING):
                        v = w_down[int(name[-1])]
                        rowsv = v[bass.ds(r * (RING * P) + s * P, P), bass.ds(h * HALF, HALF)]
                        load(sp, h * (kt // RING) + r + TURN[name], s,
                             [rowsv[:, n * BANK:(n + 1) * BANK] for n in range(2)])

        class Norm:
            def __init__(self, n):
                self.n = n
                self.bank_done = sem(f"bank_done{n}")
                self.summed = sem(f"summed{n}")
                self.stats = sem(f"stats{n}")
                self.small = sem(f"small{n}")
                self.std = sem(f"std{n}")
                self.centred = sem(f"centred{n}")
                self.turned = sem(f"turned{n}")
                self.affine_v, self.affine_a = sem(f"affine_v{n}"), sem(f"affine_a{n}")
                self.hi = sem(f"xT_hi{n}")
                self.lo = sem(f"xT_lo{n}")
        norms = [Norm(n) for n in range(4)]
        res = sem("residual")

        class Group:
            def __init__(self, n):
                self.free = sem(f"acc_free{n}")
                self.cross = sem(f"cross{n}")
                self.taps = sem(f"taps{n}")
                self.act = sem(f"gate_act{n}")
                self.gated = sem(f"gated{n}")
                self.hi = sem(f"hT_hi{n}")
                self.lo = sem(f"hT_lo{n}")
        ffn = [Group("_up0"), Group("_up1")]
        cin = Group("_in")
        glu_done, pads_made = sem("glu_done"), sem("pads_made")

        NT = 4 * FW

        def ffn_act(a, l, g, b, t0):
            s = ffn[l]
            turn = g * 2 + t0
            a.wait_ge(chunks_done, (turn + 2) * RING)
            for side in range(2):
                a.wait_ge(s.free, g * 2 + (side + 1 + 2))
                nc.scalar.activation(cross[:, side], ps[:, 4 * b + 2 * side:4 * b + 2 * side + 2, T:2 * T],
                                     ACT.Copy).then_inc(s.cross, 1)
            splits(a, turn + 2, [3])
            splits(a, turn + 3, [0])
            a.wait_ge(s.taps, (g + 1) * NT + 1)
            a.wait_ge(s.gated, g + 1)
            nc.scalar.activation(act[:], conv[:, 0], ACT.Silu).then_inc(s.act, 1)
            splits(a, turn + 3, [1])
            a.wait_ge(s.gated, g + 2)
            nc.scalar.activation(hT[:, bass.ds(g * 2, 2), 0:T], up[:, 0], ACT.Copy).then_inc(s.hi, 1)
            splits(a, turn + 3, [2, 3])
            splits(a, turn + 4, [0, 1, 2])

        def add_cross(v, s, g, b):
            for side in range(2):
                v.wait_ge(s.cross, g * 2 + (side + 1))
                nc.vector.tensor_tensor(up[:, side], cross[:, side],
                                        ps[:, 4 * b + 2 * side:4 * b + 2 * side + 2, 0:T], ALU.add
                                        ).then_inc(s.free, 1)

        def ffn_dve(v, l, g, b, t0):
            turn = g * 2 + t0
            s = ffn[l]
            v.wait_ge(s.hi, g + 1)
            v.wait_ge(s.lo, g + 1)
            v.wait_ge(s.taps, g * NT + 1)
            add_cross(v, s, g, b)
            splits(v, turn + 2, [3])
            tiles = [(side, m) for side in range(2) for m in range(2)]
            for j in range(FW):
                for n, (side, m) in enumerate(tiles):
                    tap = ffn_taps[:, l, FW - 1 - j, bass.ds(g * 2 + (side * KF + m), 1)]
                    if j == 0:
                        v.wait_ge(s.free, g * 2 + (side + 1 + 4))
                        if n == 0:
                            v.wait_ge(s.act, g + 1)
                            v.wait_ge(s.gated, g + 1)
                        nc.vector.tensor_scalar(conv[:, side, m], up[:, side, m], tap, None, ALU.mult
                                                ).then_inc(s.taps, 1)
                    else:
                        v.wait_ge(s.taps, g * NT + (4 * j - 2 + n))
                        nc.vector.scalar_tensor_tensor(
                            out=conv[:, side, m, j:T], in0=up[:, side, m, 0:T - j], scalar=tap,
                            in1=conv[:, side, m, j:T], op0=ALU.mult, op1=ALU.add).then_inc(s.taps, 1)
            splits(v, turn + 3, [0])
            v.wait_ge(s.act, g + 2)
            v.wait_ge(s.taps, (g + 1) * NT + 1)
            nc.vector.tensor_tensor(up[:, 0], act[:], conv[:, 1], ALU.mult).then_inc(s.gated, 1)
            splits(v, turn + 3, [1])
            v.wait_ge(s.gated, g + 2)
            v.wait_ge(s.hi, g + 2)
            h = hT[:, bass.ds(g * 2, 2), :]
            nc.vector.tensor_tensor(h[:, :, T:2 * T], up[:, 0], h[:, :, 0:T].bitcast(F32), ALU.subtract
                                    ).then_inc(s.lo, 1)
            splits(v, turn + 3, [2, 3])
            splits(v, turn + 4, [0, 1, 2])

        def cin_act(a, g, b, turn0):
            s = cin
            a.wait_ge(chunks_done, (turn0 + g * 2 + 2) * RING)
            for side in range(2):
                a.wait_ge(s.free, g * 2 + (side + 1 + 2))
                nc.scalar.activation(cross[:, side], ps[:, 4 * b + 2 * side:4 * b + 2 * side + 2, T:2 * T],
                                     ACT.Copy).then_inc(s.cross, 1)
            a.wait_ge(s.free, g * 2 + 6)
            a.wait_ge(glu_done, g + 1)
            nc.scalar.activation(act[:], up[:, 1], ACT.Sigmoid).then_inc(s.act, 1)

        def cin_glu(v, g, b):
            s = cin
            v.wait_ge(s.act, g + 1)
            v.wait_ge(glu_done, g + 1)
            add_cross(v, s, g, b)
            v.wait_ge(s.act, g + 2)
            v.wait_ge(s.free, g * 2 + 6)
            v.wait_ge(s.taps, g * (2 * CW) + 1)
            nc.vector.tensor_tensor(glu[:, :, CW - 1:], up[:, 0], act[:], ALU.mult).then_inc(glu_done, 1)

        def cin_tap(v, g, j):
            s = cin
            for m in range(2):
                tap = conv_taps[:, bass.ds(g * 2 + m, 1), j]
                o = conv_out[:, bass.ds(g * 2 + m, 1), :]
                i = glu[:, m:m + 1, j:j + T]
                if j == 0:
                    v.wait_ge(glu_done, g + 2)
                    nc.vector.tensor_scalar(o, i, tap, None, ALU.mult).then_inc(s.taps, 1)
                else:
                    v.wait_ge(s.taps, g * (2 * CW) + (2 * j + m))
                    nc.vector.scalar_tensor_tensor(out=o, in0=i, scalar=tap, in1=o, op0=ALU.mult, op1=ALU.add
                                                   ).then_inc(s.taps, 1)

        def bank_complete(v, s, name, kt, h, b):
            if b < 3:
                v.wait_ge(s.bank_done, 3 * h + b + 1)
            else:
                v.wait_ge(chunks_done, TURN[name] * RING + kt * (h + 1))

        def add_residual(v, n, name, kt, h):
            s = norms[n]
            for b in range(4):
                tok, c = b // 2, h * 2 + b % 2
                cols = x[:, tok, c * BANK:(c + 1) * BANK]
                bank_complete(v, s, name, kt, h, b)
                nc.vector.scalar_tensor_tensor(out=cols, in0=cols, scalar=ALPHA, in1=ps[:, b, :],
                                               op0=ALU.mult, op1=ALU.add).then_inc(s.summed, 1)
                if b > 0:
                    stat(v, s, h, b - 1)
            stat(v, s, h, 3)

        def stat(v, s, h, b):
            tok, c = b // 2, h * 2 + b % 2
            v.wait_ge(s.summed, 4 * h + b + 2)
            nc.vector.bn_stats(stats[:, tok, c, :], x[:, tok, c * BANK:(c + 1) * BANK]).then_inc(s.stats, 1)

        def deviation(v, small, std_sem, stats_sem, n_stats, step=0):
            v.wait_ge(stats_sem, n_stats)
            for tok in range(TT):
                nc.vector.bn_aggr(mv[:, tok, :], stats[:, tok]).then_inc(small, 1)
            v.wait_ge(small, 2)
            nc.vector.tensor_scalar(var_eps[:], mv[:, :, 1], EPS, None, ALU.add).then_inc(small, 1)
            v.wait_ge(std_sem, 1)
            nc.vector.reciprocal(rstd[:, 1], std[:]).then_inc(small, 1)
            v.wait_ge(small, 4)
            nc.vector.tensor_tensor(newton[:, 0], rstd[:, 1], rstd[:, 1], ALU.mult).then_inc(small, 1)
            v.wait_ge(small, 5)
            nc.vector.tensor_tensor(newton[:, 1], newton[:, 0], var_eps[:], ALU.mult).then_inc(small, 1)
            v.wait_ge(small, 6)
            nc.vector.tensor_scalar(newton[:, 2], newton[:, 1], -0.5, 1.5, ALU.mult, ALU.add).then_inc(small, 1)
            v.wait_ge(small, 7)
            nc.vector.tensor_tensor(rstd[:, 0], rstd[:, 1], newton[:, 2], ALU.mult).then_inc(small, 1)
            v.wait_ge(small, 8)

        def root(a, small, std_sem):
            a.wait_ge(small, 3)
            nc.scalar.activation(std[:], var_eps[:], ACT.Sqrt).then_inc(std_sem, 1)

        def centre(v, n):
            s = norms[n]
            for c in range(4):
                for tok in range(TT):
                    cols = x[:, tok, c * BANK:(c + 1) * BANK]
                    nc.vector.tensor_scalar(cols, cols, mv[:, tok, 0:1], rstd[:, 0, tok:tok + 1],
                                            ALU.subtract, ALU.mult).then_inc(s.centred, 1)

        def turn_pe(pe, n):
            s = norms[n]

            def job(j):
                pe.wait_ge(s.centred, 2 * (j // 2 + 1))
                if j >= 4:
                    pe.wait_ge((s.affine_v, s.affine_a)[j % 2], 2 * ((j - 4) // 2) + 2)
                turn_job(pe, 4 + j % 4, j).then_inc(s.turned, 1)

            def before(c):
                for j in (range(4) if c == 0 else range(2 * c + 2, 2 * c + 4) if c < 3 else []):
                    job(j)
                pe.wait_ge(s.lo, c + 1)
            return before

        def turn_job(pe, bank, j):
            for kk in range(2):
                for tok in range(TT):
                    k = 2 * j + kk
                    mm = nc.tensor.transpose(ps[:, bank, kk * T + tok * P:kk * T + (tok + 1) * P],
                                             x[:, tok, k * P:(k + 1) * P], ident[:])
            return mm

        def affine(eng, n, j):
            s = norms[n]
            eng.wait_ge(s.turned, j + 1)
            if j >= 2:
                eng.wait_ge(s.hi, j - 1)
                eng.wait_ge(s.lo, j - 1)
            for kk in range(2):
                k = 2 * j + kk
                src = ps[:, 4 + j % 4, kk * T:(kk + 1) * T]
                gain, bias = norm_cols[:, n, k:k + 1], norm_cols[:, 4 + n, k:k + 1]
                if j % 2:
                    mm = nc.scalar.activation(turned[:, 1, kk], src, ACT.Identity, bias=bias, scale=gain)
                else:
                    mm = nc.vector.tensor_scalar(turned[:, 0, kk], src, gain, bias, ALU.mult, ALU.add)
                mm.then_inc((s.affine_v, s.affine_a)[j % 2], 1)

        def turn_dve(v, n, split):
            s = norms[n]

            def low(j):
                v.wait_ge(s.hi, j + 1)
                hi = xT[:, 2 * j:2 * j + 2, 0:T].bitcast(F32)
                nc.vector.tensor_tensor(xT[:, 2 * j:2 * j + 2, T:2 * T], turned[:, j % 2], hi,
                                        ALU.subtract).then_inc(s.lo, 1)

            affine(v, n, 0)
            for j in range(KD // 2):
                if j % 2 and j + 1 < KD // 2:
                    affine(v, n, j + 1)
                low(j)
                if j == 2:
                    split()

        def turn_act(a, n, split):
            s = norms[n]
            for j in range(KD // 2):
                if j % 2 == 0:
                    affine(a, n, j + 1)
                a.wait_ge((s.affine_v, s.affine_a)[j % 2], 2 * (j // 2) + 2)
                nc.scalar.activation(xT[:, 2 * j:2 * j + 2, 0:T], turned[:, j % 2], ACT.Copy).then_inc(s.hi, 1)
                if j == 1:
                    split()

        def residual_piece(v, n, c):
            if c == 0:
                v.wait_ge(rows_landed[n], 32)
            for tok in range(TT):
                cols = x[:, tok, c * BANK:(c + 1) * BANK]
                nc.vector.tensor_tensor(cols, cols, rows[:, 0, c * BANK:(c + 1) * BANK], ALU.mult
                                        ).then_inc(res, 1)
            for tok in range(TT):
                cols = x[:, tok, c * BANK:(c + 1) * BANK]
                v.wait_ge(res, n * 16 + 4 * c + tok + 1)
                nc.vector.tensor_tensor(cols, cols, rows[:, 1, c * BANK:(c + 1) * BANK], ALU.add
                                        ).then_inc(res, 1)

        def half_phase(eng, name, kt, after_half, update=None, ahead=True, done=RING):
            n = kt // RING
            for h in range(2):
                first = TURN[name] + h * n
                more = ahead or h == 0
                at = done if h == 0 else RING
                turn = first + at // RING
                if at % RING:
                    splits(eng, turn, range(at % RING, RING))
                    turn += 1
                if update is not None and h == 0:
                    if done == RING:
                        splits(eng, turn)
                        turn += 1
                    for s in range(RING):
                        update(s)
                        splits(eng, turn, [s])
                    turn += 1
                split_turns(eng, turn, first + n - turn)
                if more:
                    splits(eng, first + n, range(RING - 1))
                after_half(h, lambda: splits(eng, first + n, [RING - 1]) if more else None)

        k_tok_done, rotated, qk_turned, qk_ready = sem("k_tok_done"), sem("rotated"), sem("qk_turned"), sem("qk_ready")
        rot_step, copied, q_done = sem("rot_step"), sem("copied"), sem("q_done")
        sc_done, sc_masked, mx_step, neg_max = sem("sc_done"), sem("sc_masked"), sem("mx_step"), sem("neg_max")
        exp_done, den_step, norm_done = sem("exp_done"), sem("den_step"), sem("norm_done")
        pT_turned, pT_ready, o_done, o_hi, o_lo = (sem("pT_turned"), sem("pT_ready"), sem("o_done"), sem("o_hi"),
                                                   sem("o_lo"))
        UNITS = [(n, t) for n in range(NKV) for t in range(TT)]

        def width(t):
            return (t + 1) * P

        def psum_scores(u):
            t = UNITS[u][1]
            b = 2 * (u % 2)
            v = ps[:, b:b + 1 + t, :]
            return v.rearrange("p b (g k) -> p (b g) k", k=width(t))

        def rotate(v, view, tok, i):
            h = view.shape[1]
            c = rope_sb[:, tok, 0:ROT].unsqueeze(1).broadcast_to([P, h, ROT])
            s = rope_sb[:, tok, ROT:2 * ROT].unsqueeze(1).broadcast_to([P, h, ROT])
            v.wait_ge(copied, i + 1)
            if i >= 1:
                v.wait_ge(rotated, i)
            nc.vector.tensor_tensor(rot[:, 0, 0:h], view[:, :, 0:ROT], c, ALU.mult).then_inc(rot_step, 1)
            nc.vector.tensor_tensor(rot[:, 1, 0:h, 0:RH], view[:, :, RH:ROT], s[:, :, 0:RH], ALU.mult
                                    ).then_inc(rot_step, 1)
            nc.vector.tensor_tensor(rot[:, 1, 0:h, RH:ROT], view[:, :, 0:RH], s[:, :, RH:ROT], ALU.mult
                                    ).then_inc(rot_step, 1)
            v.wait_ge(rot_step, 3 * (i + 1))
            nc.vector.tensor_tensor(view[:, :, 0:ROT], rot[:, 0, 0:h], rot[:, 1, 0:h], ALU.add
                                    ).then_inc(rotated, 1)

        def q_view(tok, i):
            return q_tok[:, tok, i].rearrange("p g e d -> p (g e) d")

        kv_bank_done, q_bank_done, q_free = sem("kv_bank_done"), sem("q_bank_done"), sem("q_free")
        v_copied = sem("v_copied")

        c_turned, c_stats, c_small, c_std, c_shift = (sem("c_turned"), sem("c_stats"), sem("c_small"), sem("c_std"),
                                                      sem("c_shift"))
        c_bcast, c_scaled, c_norm, c_silu, s_hi, s_lo = (sem("c_bcast"), sem("c_scaled"), sem("c_norm"),
                                                         sem("c_silu"), sem("s_hi"), sem("s_lo"))

        block = ctx.enter_context(nc.Block())

        @block.sync
        def _(sp):
            for i in range(4):
                for tok in range(TT):
                    sp.dma_start(x[:, tok, i * BANK:(i + 1) * BANK],
                                 x_in[0, tok * P:(tok + 1) * P, i * BANK:(i + 1) * BANK]
                                 ).then_inc(x_landed[i], 16)
            for name in ("wk", "wv"):
                for j in range(KD // 2):
                    load(sp, TURN[name] + j // RING, j % RING,
                         [w_view[name][:, 2 * j + kk, :] for kk in range(2)])
            half_loads(sp, "wq", KD)
            half_loads(sp, "wo", KD)
            group_loads(sp, "up0", KF // 2)
            half_loads_k(sp, "down0", KF)
            group_loads(sp, "w_in", KD // 2)
            half_loads(sp, "w_out", KD)
            group_loads(sp, "up1", KF // 2)
            half_loads_k(sp, "down1", KF)
            for c in range(4):
                sp.wait_ge(res, 3 * 16 + 4 * (c + 1))
                for tok in range(TT):
                    sp.dma_start(out[0, tok * P:(tok + 1) * P, c * BANK:(c + 1) * BANK],
                                 x[:, tok, c * BANK:(c + 1) * BANK]).then_inc(stored, 16)
            sp.wait_ge(stored, 16 * 4 * TT)

        @block.gpsimd
        def _(pool):
            nc.gpsimd.memset(ident[:], 1.0).then_inc(ident_made, 1)
            pool.wait_ge(ident_made, 1)
            nc.gpsimd.affine_select(out=ident[:], in_=ident[:], compare_op=ALU.is_equal, fill=0.0, base=0,
                                    pattern=[[-1, P]], channel_multiplier=1).then_inc(ident_made, 1)
            for i, v in enumerate((norm_g, norm_b)):
                pool.dma_start(norm_rows[64 * i:64 * (i + 1), :], v.rearrange("l s (t p) -> (l s t) p", p=P)
                               ).then_inc(vectors_landed, 16)
            for i, v in enumerate((conv_g, conv_b)):
                pool.dma_start(convn_rows[KD * i:KD * (i + 1), :], v[0].rearrange("(t p) -> t p", p=P)
                               ).then_inc(vectors_landed, 16)
            for l in range(DEPTH):
                pool.dma_start(tap_rows[:, l], ffn_dw[l].rearrange("j (t p) -> t j p", p=P)
                               ).then_inc(vectors_landed, 16)
            pool.dma_start(dw_rows[:], conv_dw[0]).then_inc(vectors_landed, 16)
            pool.dma_start(rope_sb[:], rope.rearrange("(t p) c -> p t c", p=P)).then_inc(rope_landed, 16)
            pool.dma_start(sink[:], broadcast_rows(sinks)).then_inc(sink_landed, 16)
            for n, name in ((0, "down0"), (1, "w_out"), (2, "down1")):
                pool.wait_ge(chunks_done, TURN[name] * RING)
                for i, v in enumerate((norm_g, norm_b)):
                    pool.dma_start(rows[:, i, :], broadcast_rows(v[n // 2, n % 2:n % 2 + 1])
                                   ).then_inc(rows_landed[n], 16)
                if n == 0:
                    pool.wait_ge(lo_ready, (TURN["w_in"] + 1) * RING)
                    with pool.Fori(0, TURN["w_out"] - TURN["w_in"]) as r:
                        for slot in range(RING):
                            take_lo(pool, r + TURN["w_in"] + 1, slot)
            pool.wait_ge(res, 3 * 16)
            for i, v in enumerate((norm_g, norm_b)):
                pool.dma_start(rows[:, i, :], broadcast_rows(v[1, 1:2])).then_inc(rows_landed[3], 16)

        @block.scalar
        def _(a):
            SPLIT["act"] = a
            for s in (ffn[0].act, ffn[0].hi, ffn[1].act, ffn[1].hi, cin.act):
                a.sem_inc(s, 1)
            for j in range(KD // 2):
                a.wait_ge(x_turned, j + 1)
                nc.scalar.activation(xT[:, 2 * j:2 * j + 2, 0:T],
                                     ps[:, j % 4, :].rearrange("p (k t) -> p k t", k=2), ACT.Copy
                                     ).then_inc(x_hi, 1)
                if j < RING:
                    round_hi(a, 0, j)
            for t in range(1, TURN["wq"] + 1):
                if t == TURN["wq"]:
                    splits(a, t, range(RING - 1))
                    for tok in range(TT):
                        if tok == 0:
                            a.wait_ge(kv_bank_done, 2)
                        else:
                            a.wait_ge(chunks_done, TURN["wq"] * RING)
                        nc.scalar.activation(v_tok[:, tok], ps[:, 2 + tok, :], ACT.Copy).then_inc(v_copied, 1)
                    splits(a, t, [RING - 1])
                else:
                    splits(a, t)
                    if t == TURN["wv"]:
                        for tok in range(TT):
                            if tok == 0:
                                a.wait_ge(kv_bank_done, 1)
                            else:
                                a.wait_ge(chunks_done, TURN["wv"] * RING)
                            nc.scalar.activation(k_tok[:, tok], ps[:, tok, :], ACT.Copy).then_inc(copied, 1)

            def q_out(h, split):
                for b in range(4):
                    tok, i = b // 2, 2 * h + b % 2
                    if b < 3:
                        a.wait_ge(q_bank_done, 3 * h + b + 1)
                    else:
                        a.wait_ge(chunks_done, TURN["wq"] * RING + KD * (h + 1))
                    nc.scalar.activation(q_tok[:, tok, i].rearrange("p g e d -> p e g d"),
                                         ps[:, b, :].rearrange("p (e g d) -> p e g d", e=2, g=GR),
                                         ACT.Copy).then_inc(copied, 1)
                split()

            half_phase(a, "wq", KD, q_out)
            for i in range(10):
                a.wait_ge(qk_turned, i + 1)
                if i < 2:
                    to = kT[:, :, i * P:(i + 1) * P]
                else:
                    h, b = (i - 2) // 4, (i - 2) % 4
                    tok, kv = b // 2, 2 * h + b % 2
                    to = qT[:, kv * GR:(kv + 1) * GR, tok * P:(tok + 1) * P]
                nc.scalar.activation(to, ps[:, 4 + i % 4, :].rearrange("p (g t) -> p g t", g=4), ACT.Copy
                                     ).then_inc(qk_ready, 1)

            def exps(u):
                t = UNITS[u][1]
                a.wait_ge(neg_max, u + 1)
                if u >= 2:
                    a.wait_ge(pT_turned, u - 1)
                for g in range(GR):
                    nc.scalar.activation(probs[:, u % 2, g, 0:width(t)], scores[:, u % 2, g, 0:width(t)],
                                         ACT.Exp, bias=smalls[:, u % 2, 2, g:g + 1],
                                         accum_out=smalls[:, u % 2, 4, g:g + 1]).then_inc(exp_done, 1)
                nc.scalar.activation(smalls[:, u % 2, 5], smalls[:, u % 2, 3], ACT.Exp).then_inc(exp_done, 1)

            exps(0)
            for u, (n, t) in enumerate(UNITS):
                if u + 1 < len(UNITS):
                    exps(u + 1)
                a.wait_ge(pT_turned, u + 1)
                if u >= 2:
                    a.wait_ge(o_done, u - 1)
                b = (t + 1) * GR
                nc.scalar.activation(probsT[:, u % 2, 0:b, :],
                                     ps[:, 4:5 + t, :].rearrange("p b (g q) -> p (b g) q", q=P), ACT.Copy
                                     ).then_inc(pT_ready, 1)
                a.wait_ge(o_done, u + 1)
                nc.scalar.activation(hT[:, 2 * n:2 * n + 2, t * P:(t + 1) * P],
                                     ps[:, 6 + u % 2, 0:2 * P].rearrange("p (j q) -> p j q", j=2), ACT.Copy
                                     ).then_inc(o_hi, 1)

            def norm_act(n):
                def after(h, split):
                    if h == 1:
                        root(a, norms[n].small, norms[n].std)
                        turn_act(a, n, split)
                    else:
                        split()
                return after

            half_phase(a, "wo", KD, norm_act(0))

            def ffn_phase(l):
                t0 = TURN[f"up{l}"]
                splits(a, t0 + 1)
                splits(a, t0 + 2, range(RING - 1))
                nc.scalar.preload_act_table(ACT.Silu)
                with a.Fori(0, KF // 4) as pair:
                    for b in range(2):
                        ffn_act(a, l, pair * 2 + b, b, t0)

            ffn_phase(0)
            half_phase(a, "down0", KF, norm_act(1), done=11)
            t0 = TURN["w_in"]
            with a.Fori(0, KD // 4) as pair:
                for b in range(2):
                    g = pair * 2 + b
                    splits(a, g * 2 + (t0 + 1))
                    splits(a, g * 2 + (t0 + 2), range(RING - 1))
                    cin_act(a, g, b, t0)
                    splits(a, g * 2 + (t0 + 2), [RING - 1])
            root(a, c_small, c_std)
            for j in range(KD // 2):
                a.wait_ge(c_norm, j + 1)
                for kk in range(2):
                    k = 2 * j + kk
                    if j >= 1:
                        a.wait_ge(s_lo, j)
                    nc.scalar.activation(silu_out[:, kk], conv_out[:, k], ACT.Silu, bias=conv_cols[:, 1, k:k + 1],
                                         scale=conv_cols[:, 0, k:k + 1]).then_inc(c_silu, 1)
                a.wait_ge(c_silu, 2 * j + 2)
                nc.scalar.activation(hT[:, 2 * j:2 * j + 2, 0:T], silu_out[:], ACT.Copy).then_inc(s_hi, 1)
            half_phase(a, "w_out", KD, norm_act(2))
            ffn_phase(1)

            def last(h, split):
                if h == 1:
                    root(a, norms[3].small, norms[3].std)
                split()
            half_phase(a, "down1", KF, last, ahead=False, done=11)

        @block.vector
        def _(v):
            for s in (ffn[0].taps, ffn[0].gated, ffn[0].lo, ffn[1].taps, ffn[1].gated, ffn[1].lo, cin.taps,
                      glu_done, norms[0].summed, norms[1].summed, norms[2].summed, norms[3].summed):
                v.sem_inc(s, 1)
            nc.vector.memset(mask[:], MASKED).then_inc(mask_made, 1)
            v.wait_ge(mask_made, 1)
            for part, lo, hi in ((0, 0, CHUNK), (64, 0, P), (0, P + CHUNK, P + 3 * CHUNK), (64, 2 * P, 2 * P + P)):
                nc.vector.memset(mask[part:part + CHUNK, lo:hi], 0.0).then_inc(mask_made, 1)
            for j in range(KD // 2):
                v.wait_ge(x_hi, j + 1)
                nc.vector.tensor_tensor(xT[:, 2 * j:2 * j + 2, T:2 * T],
                                        ps[:, j % 4, :].rearrange("p (k t) -> p k t", k=2),
                                        xT[:, 2 * j:2 * j + 2, 0:T].bitcast(F32), ALU.subtract).then_inc(x_lo, 1)
                if j < RING:
                    take_lo(v, 0, j)
            v.wait_ge(vectors_turned, 4)
            nc.vector.tensor_copy(norm_cols[:].rearrange("p a t -> p (a t)"), ps[:, 4, 0:P]).then_inc(vectors_ready, 1)
            nc.vector.tensor_copy(conv_cols[:].rearrange("p a t -> p (a t)"), ps[:, 4, P:P + 2 * KD]
                                  ).then_inc(vectors_ready, 1)
            for l in range(DEPTH):
                nc.vector.tensor_copy(ffn_taps[:, l].rearrange("p j t -> p (j t)"), ps[:, 5 + l, 0:FW * 2 * KF]
                                      ).then_inc(vectors_ready, 1)
            nc.vector.tensor_copy(conv_taps[:].rearrange("p t j -> p (t j)"), ps[:, 7, 0:KD * CW]
                                  ).then_inc(vectors_ready, 1)
            split_turns_from = 1
            for t in range(1, TURN["wq"] + 1):
                splits(v, t, range(RING - 1))
                if t == TURN["wv"] + 1:
                    v.wait_ge(rope_landed, 16)
                    for tok in range(TT):
                        rotate(v, k_tok[:, tok].rearrange("p (h d) -> p h d", d=HD), tok, tok)
                splits(v, t, [RING - 1])

            def q_rot(h, split):
                for b in range(4):
                    tok, i = b // 2, 2 * h + b % 2
                    rotate(v, q_view(tok, i), tok, 2 + 4 * h + b)
                    if b == 1:
                        split()

            half_phase(v, "wq", KD, q_rot)

            def masked(u):
                n, t = UNITS[u]
                w = width(t)
                sm = smalls[:, u % 2]
                v.wait_ge(sc_done, u + 1)
                if u >= 2:
                    v.wait_ge(exp_done, 5 * (u - 1))
                    v.wait_ge(neg_max, u - 1)
                m = mask[:, t * P:t * P + w].unsqueeze(1).broadcast_to([P, GR, w])
                nc.vector.scalar_tensor_tensor(out=scores[:, u % 2, :, 0:w], in0=psum_scores(u), scalar=SCALE,
                                               in1=m, op0=ALU.mult, op1=ALU.add).then_inc(sc_masked, 1)
                v.wait_ge(sc_masked, u + 1)
                nc.vector.tensor_reduce(sm[:, 0], scores[:, u % 2, :, 0:w], AX.X, ALU.max).then_inc(mx_step, 1)
                v.wait_ge(mx_step, 3 * u + 1)
                nc.vector.tensor_tensor(sm[:, 1], sm[:, 0], sink[:, n * GR:(n + 1) * GR], ALU.max
                                        ).then_inc(mx_step, 1)
                v.wait_ge(mx_step, 3 * u + 2)
                nc.vector.tensor_tensor(sm[:, 3], sink[:, n * GR:(n + 1) * GR], sm[:, 1], ALU.subtract
                                        ).then_inc(mx_step, 1)
                v.wait_ge(mx_step, 3 * u + 3)
                nc.vector.tensor_scalar(sm[:, 2], sm[:, 1], -1.0, None, ALU.mult).then_inc(neg_max, 1)

            def normalise(u):
                n, t = UNITS[u]
                sm = smalls[:, u % 2]
                v.wait_ge(exp_done, 5 * (u + 1))
                nc.vector.tensor_tensor(sm[:, 6], sm[:, 4], sm[:, 5], ALU.add).then_inc(den_step, 1)
                v.wait_ge(den_step, 2 * u + 1)
                if u >= 2:
                    v.wait_ge(norm_done, GR * (u - 1))
                nc.vector.reciprocal(sm[:, 7], sm[:, 6]).then_inc(den_step, 1)
                v.wait_ge(den_step, 2 * u + 2)
                for g in range(GR):
                    p = probs[:, u % 2, g, 0:width(t)]
                    nc.vector.tensor_scalar(p, p, sm[:, 7, g:g + 1], None, ALU.mult).then_inc(norm_done, 1)

            v.wait_ge(sink_landed, 16)
            v.wait_ge(mask_made, 5)
            masked(0)
            for u, (n, t) in enumerate(UNITS):
                if u + 1 < len(UNITS):
                    masked(u + 1)
                normalise(u)
                v.wait_ge(o_hi, u + 1)
                nc.vector.tensor_tensor(hT[:, 2 * n:2 * n + 2, T + t * P:T + (t + 1) * P],
                                        ps[:, 6 + u % 2, 0:2 * P].rearrange("p (j q) -> p j q", j=2),
                                        hT[:, 2 * n:2 * n + 2, t * P:(t + 1) * P].bitcast(F32), ALU.subtract
                                        ).then_inc(o_lo, 1)

            def norm_dve(n, name, kt, free=None):
                def after(h, split):
                    add_residual(v, n, name, kt, h)
                    if h == 0 or n == 3:
                        split()
                    if h == 1:
                        s = norms[n]
                        if free is not None:
                            v.wait_ge(s.summed, 9)
                            v.sem_inc(free, 2)
                        deviation(v, s.small, s.std, s.stats, 8)
                        centre(v, n)
                        if n < 3:
                            turn_dve(v, n, split)
                            v.wait_ge(s.affine_a, KD // 2)
                            v.wait_ge(s.affine_v, KD // 2)
                            v.sem_inc(free, 2)
                return after

            half_phase(v, "wo", KD, norm_dve(0, "wo", KD, ffn[0].free))

            def ffn_phase(l):
                t0 = TURN[f"up{l}"]
                splits(v, t0 + 1)
                splits(v, t0 + 2, range(RING - 1))
                with v.Fori(0, KF // 4) as pair:
                    for b in range(2):
                        ffn_dve(v, l, pair * 2 + b, b, t0)

            ffn_phase(0)
            half_phase(v, "down0", KF, norm_dve(1, "down0", KF, cin.free),
                       update=lambda c: residual_piece(v, 0, c), done=11)
            nc.vector.memset(glu[:, :, 0:CW - 1], 0.0).then_inc(pads_made, 1)
            v.wait_ge(pads_made, 1)
            t0 = TURN["w_in"]
            with v.Fori(0, KD // 4) as pair:
                for b in range(2):
                    g = pair * 2 + b
                    cin_glu(v, g, b)
                    for j in range(CW):
                        cin_tap(v, g, j)
            for i in range(8):
                tok, c = i // 4, i % 4
                v.wait_ge(c_turned, i + 1)
                nc.vector.bn_stats(stats[:, tok, c, :], ps[:, i, :]).then_inc(c_stats, 1)
            deviation(v, c_small, c_std, c_stats, 8)
            nc.vector.tensor_tensor(newton[:, 0], mv[:, :, 0], rstd[:, 0], ALU.mult).then_inc(c_small, 1)
            v.wait_ge(c_small, 9)
            nc.vector.tensor_scalar(shift[:], newton[:, 0], -1.0, None, ALU.mult).then_inc(c_shift, 1)
            v.wait_ge(c_bcast, 1)

            def c_step(j):
                o = conv_out[:, 2 * j:2 * j + 2]
                nc.vector.tensor_tensor(o, o, ps[:, 4, 0:T].unsqueeze(1).broadcast_to([P, 2, T]), ALU.mult
                                        ).then_inc(c_scaled, 1)
                v.wait_ge(c_scaled, j + 1)
                nc.vector.tensor_tensor(o, o, ps[:, 4, T:2 * T].unsqueeze(1).broadcast_to([P, 2, T]), ALU.add
                                        ).then_inc(c_norm, 1)
            c_step(0)
            for j in range(KD // 2):
                if j + 1 < KD // 2:
                    c_step(j + 1)
                v.wait_ge(s_hi, j + 1)
                nc.vector.tensor_tensor(hT[:, 2 * j:2 * j + 2, T:2 * T], silu_out[:],
                                        hT[:, 2 * j:2 * j + 2, 0:T].bitcast(F32), ALU.subtract).then_inc(s_lo, 1)
            v.wait_ge(lo_ready, (TURN["w_out"] + 1) * RING)
            half_phase(v, "w_out", KD, norm_dve(2, "w_out", KD, ffn[1].free),
                       update=lambda c: residual_piece(v, 1, c))
            ffn_phase(1)
            half_phase(v, "down1", KF, norm_dve(3, "down1", KF), update=lambda c: residual_piece(v, 2, c),
                       ahead=False, done=11)
            v.wait_ge(norms[3].centred, 8)
            for c in range(4):
                residual_piece(v, 3, c)

        @block.tensor
        def _(pe):
            pe.wait_ge(ident_made, 2)
            for j in range(KD // 2):
                if j % 2 == 0:
                    pe.wait_ge(x_landed[j // 2], 32)
                if j >= 4:
                    pe.wait_ge(x_lo, j - 3)
                turn_job(pe, j % 4, j).then_inc(x_turned, 1)
            pe.wait_ge(vectors_landed, 16 * 7)
            nc.tensor.transpose(ps[:, 4, 0:P], norm_rows[:], ident[:])
            nc.tensor.transpose(ps[:, 4, P:P + 2 * KD], convn_rows[:], ident[0:2 * KD, 0:2 * KD]
                                ).then_inc(vectors_turned, 1)
            for l in range(DEPTH):
                for j in range(FW):
                    mm = nc.tensor.transpose(ps[:, 5 + l, j * 2 * KF:(j + 1) * 2 * KF], tap_rows[:, l, j, :],
                                             ident[0:2 * KF, 0:2 * KF])
                mm.then_inc(vectors_turned, 1)
            for t in range(KD):
                mm = nc.tensor.transpose(ps[:, 7, t * CW:(t + 1) * CW], dw_rows[:, t * P:(t + 1) * P],
                                         ident[0:CW, 0:CW])
            mm.then_inc(vectors_turned, 1)
            pe.wait_ge(x_lo, KD // 2)
            for i, name in enumerate(("wk", "wv")):
                for j in range(KD // 2):
                    parts = [(2 * i + tok, tok, [(2 * j, 0), (2 * j + 1, BANK)]) for tok in range(TT)]
                    rows_chunk(pe, TURN[name] + j // RING, j % RING, xT, parts, j == 0, j == KD // 2 - 1,
                               None, kv_bank_done)
            pe.wait_ge(copied, 2)
            pe.wait_ge(v_copied, 2)
            with pe.Fori(0, 2) as h:
                for k in range(KD):
                    turn = h * (KD // RING) + (TURN["wq"] + k // RING)
                    parts = [(tok * 2 + n, tok, [(k, n * BANK)]) for tok in range(TT) for n in range(2)]
                    rows_chunk(pe, turn, k % RING, xT, parts, k == 0, k == KD - 1,
                               lambda b: pe.wait_ge(copied, h * (b + 1) + 2), q_bank_done)
            pe.wait_ge(vectors_ready, 5)
            for i in range(10):
                if i >= 4:
                    pe.wait_ge(qk_ready, i - 3)
                pe.wait_ge(rotated, i + 1)
                for j in range(4):
                    if i < 2:
                        src = k_tok[:, i, j * P:(j + 1) * P]
                    else:
                        h, b = (i - 2) // 4, (i - 2) % 4
                        tok, kv = b // 2, 2 * h + b % 2
                        src = q_tok[:, tok, kv, j].rearrange("p e d -> p (e d)")
                    mm = nc.tensor.transpose(ps[:, 4 + i % 4, j * P:(j + 1) * P], src, ident[:])
                mm.then_inc(qk_turned, 1)
            pe.wait_ge(qk_ready, 10)

            def score(u):
                n, t = UNITS[u]
                e, i = n % 2, n // 2
                if u >= 2:
                    pe.wait_ge(sc_masked, u - 1)
                w = width(t)
                o = psum_scores(u)
                for g in range(GR):
                    mm = nc.tensor.matmul(o[:, g, :], qT[64 * e:64 * e + 64, i * GR + g, t * P:(t + 1) * P],
                                          kT[64 * e:64 * e + 64, i, 0:w], start=True, stop=True)
                mm.then_inc(sc_done, 1)

            score(0)
            score(1)
            for u, (n, t) in enumerate(UNITS):
                pe.wait_ge(norm_done, GR * (u + 1))
                if u >= 1:
                    pe.wait_ge(pT_ready, u)
                pt = ps[:, 4:5 + t, :].rearrange("p b (g q) -> p (b g) q", q=P)
                for g in range(GR):
                    for kb in range(t + 1):
                        mm = nc.tensor.transpose(pt[:, g * (t + 1) + kb, :], probs[:, u % 2, g, kb * P:(kb + 1) * P],
                                                 ident[:])
                mm.then_inc(pT_turned, 1)
                if u + 2 < len(UNITS):
                    score(u + 2)
                pe.wait_ge(pT_ready, u + 1)
                if u >= 2:
                    pe.wait_ge(o_lo, u - 1)
                for g in range(GR):
                    r = 64 * (g % 2)
                    o = ps[r:r + 64, 6 + u % 2, (g // 2) * P:(g // 2 + 1) * P]
                    for kb in range(t + 1):
                        mm = nc.tensor.matmul(o, v_tok[:, kb, n * HD:(n + 1) * HD],
                                              probsT[:, u % 2, g * (t + 1) + kb, :], start=(kb == 0), stop=(kb == t))
                mm.then_inc(o_done, 1)
            pe.wait_ge(o_lo, len(UNITS))
            halves(pe, "wo", hT, KD, norms[0].summed, norms[0].bank_done)
            groups(pe, "up0", KF // 2, ffn[0].free, turn_pe(pe, 0))
            pe.wait_ge(ffn[0].free, 4 + KF - 2)
            halves(pe, "down0", hT, KF, norms[1].summed, norms[1].bank_done, (ffn[0].lo, 1))
            groups(pe, "w_in", KD // 2, cin.free, turn_pe(pe, 1))
            for i in range(8):
                tok, c = i // 4, i % 4
                if i < 4:
                    pe.wait_ge(cin.taps, (2 * c + 2) * 2 * CW + 1)
                if i == 0:
                    pe.wait_ge(cin.free, 4 + KD)
                for j in range(4):
                    mm = nc.tensor.transpose(ps[:, i, j * P:(j + 1) * P],
                                             conv_out[:, 4 * c + j, tok * P:(tok + 1) * P], ident[:])
                mm.then_inc(c_turned, 1)
            pe.wait_ge(c_shift, 1)
            for i, col in enumerate((rstd[:, 0], shift[:])):
                for tok in range(TT):
                    mm = nc.tensor.matmul(ps[:, 4, i * T + tok * P:i * T + (tok + 1) * P],
                                          col[:, tok:tok + 1].broadcast_to([P, P]), ident[:], start=True, stop=True)
            mm.then_inc(c_bcast, 1)
            halves(pe, "w_out", hT, KD, norms[2].summed, norms[2].bank_done, (s_lo, 0))
            pe.wait_ge(c_norm, KD // 2)
            groups(pe, "up1", KF // 2, ffn[1].free, turn_pe(pe, 2))
            pe.wait_ge(ffn[1].free, 4 + KF - 2)
            halves(pe, "down1", hT, KF, norms[3].summed, norms[3].bank_done, (ffn[1].lo, 1))


def ARENA_START(nc, arena):
    return 16512


_INS = ["x", "attn_wq", "attn_wk", "attn_wv", "attn_wo", "attn_sinks", "conv_w_in", "conv_dw", "conv_norm_g",
        "conv_norm_b", "conv_w_out", "ffn_w_up", "ffn_dw", "ffn_w_down", "norm_g", "norm_b"]


def rope_table():
    inv = np.float32(500000.0) ** (-np.arange(0, ROT, 2, dtype=np.float32) / np.float32(ROT))
    ang = np.arange(T, dtype=np.float32)[:, None] * inv.astype(np.float32)[None, :]
    c, s = np.cos(ang).astype(np.float32), np.sin(ang).astype(np.float32)
    return np.ascontiguousarray(np.concatenate([c, c, -s, s], axis=1))


def kernel(**inputs):
    import numpy as _np
    import concourse.bacc as _bacc
    from concourse import mybir as _mybir
    from concourse.bass_utils import run_bass_kernel_spmd as _run

    nc = _bacc.Bacc("TRN2", target_bir_lowering=False, num_devices=1)
    arrays, args = {}, []
    for name in _INS:
        a = _np.ascontiguousarray(inputs[name])
        arrays[f"in_{name}_dram"] = a
        args.append(nc.dram_tensor(f"in_{name}_dram", a.shape, _mybir.dt.from_np(a.dtype), kind="ExternalInput").ap())
    table = rope_table()
    arrays["rope_dram"] = table
    args.append(nc.dram_tensor("rope_dram", table.shape, _mybir.dt.from_np(table.dtype), kind="ExternalInput").ap())
    args.append(nc.dram_tensor("out_dram", (1, T, D), _mybir.dt.from_np(_np.dtype("float32")),
                               kind="ExternalOutput").ap())
    trunk(nc, *args)
    r = _run(nc, [arrays], core_ids=[0])
    return r.results[0]["out_dram"]
```

```python
from contextlib import ExitStack

import numpy as np

import concourse.bass as bass
from concourse import mybir

ACT = mybir.ActivationFunctionType
ALU = mybir.AluOpType
AX = mybir.AxisListType
F32 = mybir.dt.float32
F32R = mybir.dt.float32r

P = 128
T = 256
TT = T // P
D = 2048
KD = D // P
F = 5632
KF = F // P
HD = 64
NH = D // HD
NKV = 8
GR = NH // NKV
KVD = NKV * HD
CHUNK = 64
ROT = HD // 4
RH = ROT // 2
CW = 31
FW = 3
DEPTH = 2
EPS = 1e-5
ALPHA = (2.0 * DEPTH) ** 0.25
SCALE = HD ** -0.5
BANK = 512
RING = 4
CE = 1024
HALF = D // 2
MASKED = -1e38
AB = 4
PE_TAPS = 9
DVE_TAPS = CW - PE_TAPS
FIRST_TAPS = 7
LAST_TAPS = DVE_TAPS + FIRST_TAPS
EXTRA = 4

TURN = {}
_t = 0
for _name, _elements in (("wk", D * KVD), ("wv", D * KVD), ("wq", D * D), ("wo", D * D), ("up0", D * 2 * F),
                         ("down0", F * D), ("w_in", D * 2 * D), ("w_out", D * D), ("up1", D * 2 * F),
                         ("down1", F * D)):
    TURN[_name] = _t
    _t += _elements // (P * CE * RING)
TURNS = _t


def broadcast_rows(vector, n=P):
    return bass.AP(tensor=vector.tensor, offset=vector.offset, ap=[[0, n]] + [list(d) for d in vector.ap[1:]])


def trunk(nc, x_in, wq, wk, wv, wo, sinks, w_in, conv_dw, conv_g, conv_b, w_out, w_up, ffn_dw, w_down,
          norm_g, norm_b, rope, out):
    with ExitStack() as ctx:
        sem_count = [0]

        def sem(name):
            sem_count[0] += 1
            return ctx.enter_context(nc.semaphore(name))

        ARENA = 212832
        arena = ctx.enter_context(nc.sbuf_tensor("arena", [P, ARENA // 4], F32))

        small_at = [0]
        place = [0]

        def at(name, shape, dt, offset):
            return nc.alloc_sbuf_tensor_at(name, shape, dt, offset=START + offset)


        START = ARENA_START(nc, arena)

        def put(name, shape, dt):
            size = int(np.prod(shape[1:])) * 4
            t = at(name, shape, dt, place[0])
            place[0] += (size + 31) // 32 * 32
            assert place[0] <= ARENA, (name, place[0])
            return t

        x = put("x", [P, TT, D], F32)
        XT_AT = place[0]
        xT = put("xT", [P, KD, 2 * T], F32R)
        HT_AT = place[0]
        hT = put("hT", [P, KF, 2 * T], F32R)
        raw = put("raw", [P, RING, CE], F32)
        w_hi = put("w_hi", [P, RING, CE], F32R)
        w_lo = put("w_lo", [P, RING, CE], F32R)
        ident = put("ident", [P, P], F32)
        norm_cols = put("norm_cols", [P, 2 * 2 * DEPTH, KD], F32)
        conv_cols = put("conv_cols", [P, 2, KD], F32)
        ffn_taps = put("ffn_taps", [P, DEPTH, FW, 2 * KF], F32)
        conv_taps = put("conv_taps", [P, KD, CW], F32)
        stats = put("stats", [P, TT, 4, 6], F32)
        mv = put("mv", [P, TT, 2], F32)
        var_eps = put("var_eps", [P, TT], F32)
        std = put("std", [P, TT], F32)
        rstd = put("rstd", [P, 2, TT], F32)
        newton = put("newton", [P, 3, TT], F32)
        shift = put("shift", [P, TT], F32)
        eps = put("eps", [P, 1], F32)
        turned = put("turned", [P, 2, 2, T], F32)
        cross = put("cross", [P, 2, 2, T], F32)
        up = put("up", [P, 2, 2, T], F32)
        conv = put("conv", [P, 2, 2, T], F32)
        act = put("act", [P, 2, T], F32)

        rows = at("rows", [P, 2, D], F32, XT_AT)
        probs = at("probs", [P, AB, GR, T], F32, XT_AT)
        probsT = at("probsT", [P, AB, 2 * GR, P], F32, XT_AT + 16384)
        hole = HT_AT + KD * 2 * T * 4
        q_tok = at("q_tok", [P, TT, NKV // 2, GR, 2, HD], F32, hole)
        qT = at("qT", [P, NH // 2, T], F32, hole + 16384)
        k_tok = at("k_tok", [P, TT, KVD], F32, hole + 32768)
        kT = at("kT", [P, NKV // 2, T], F32, hole + 36864)
        v_tok = at("v_tok", [P, TT, KVD], F32, hole + 40960)
        o_at = hole + 45056
        mask = at("mask", [P, P + T], F32, o_at)
        sink = at("sink", [P, NH], F32, o_at + 1536)
        rope_sb = at("rope_sb", [P, TT, 2 * ROT], F32, o_at + 1664)
        rot = at("rot", [P, 2, 8, ROT], F32, o_at + 1920)
        smalls = at("smalls", [P, AB, 8, GR], F32, o_at + 2944)
        conv_out = at("conv_out", [P, KD, T], F32, hole)
        glu = at("glu", [P, 2, CW - 1 + T], F32, hole + 16384)
        silu_out = at("silu_out", [P, 2, T], F32, hole + 16384 + 2304)
        last_diag = at("last_diag", [P, LAST_TAPS, 2, P], F32R, hole + 20736)
        diag = at("diag", [P, 2, PE_TAPS, 2, P], F32R, HT_AT)
        glu_split = at("glu_split", [P, 2, CW - 1 + T], F32R, HT_AT + PE_TAPS * 2048)
        first_split = at("first_split", [P, 2, CW - 1 + T], F32R, HT_AT + 2304 + PE_TAPS * 2048)
        taps_hi = at("taps_hi", [P, KD, CW], F32R, HT_AT + 4608 + PE_TAPS * 2048)
        taps_lo = at("taps_lo", [P, KD, CW], F32, HT_AT + 6592 + PE_TAPS * 2048)
        norm_rows = at("norm_rows", [P, P], F32, HT_AT)
        convn_rows = at("convn_rows", [2 * KD, P], F32, HT_AT + 512)
        tap_rows = at("tap_rows", [2 * KF, DEPTH, FW, P], F32, HT_AT + 1024)
        dw_rows = at("dw_rows", [CW, D], F32, HT_AT + 8192)

        ps = ctx.enter_context(nc.psum_tensor("ps", [P, 8, BANK], F32))

        raw_landed = [sem(f"raw_landed{s}") for s in range(RING)]
        hi_ready, lo_ready, chunks_done = sem("hi_ready"), sem("lo_ready"), sem("chunks_done")
        x_landed = [sem(f"x_landed{i}") for i in range(4)]
        vectors_landed, rope_landed, sink_landed = sem("vectors_landed"), sem("rope_landed"), sem("sink_landed")
        ident_made, vectors_turned, vectors_ready = sem("ident_made"), sem("vectors_turned"), sem("vectors_ready")
        x_turned, x_hi, x_lo = sem("x_turned"), sem("x_hi"), sem("x_lo")
        stored = sem("stored")
        first_known, first_centred, first_out, second_out = (sem("first_known"), sem("first_centred"),
                                                             sem("first_out"), sem("second_out"))
        first_gain = sem("first_gain")
        rows_landed = [sem(f"rows_landed{i}") for i in range(4)]
        rows_used = sem("rows_used")
        dve_const, mask_made = sem("dve_const"), sem("mask_made")

        w_view = {
            "wk": wk[0].rearrange("(k p) c -> p k c", p=P), "wv": wv[0].rearrange("(k p) c -> p k c", p=P),
            "wq": wq[0].rearrange("(k p) c -> p k c", p=P), "wo": wo[0].rearrange("(k p) c -> p k c", p=P),
            "w_out": w_out[0].rearrange("(k p) c -> p k c", p=P),
            "w_in": w_in[0].rearrange("(k p) (s c) -> p k s c", p=P, s=2),
        }
        for l in range(DEPTH):
            w_view[f"up{l}"] = w_up[l].rearrange("(k p) (s c) -> p k s c", p=P, s=2)
            w_view[f"down{l}"] = w_down[l].rearrange("(k p) c -> p k c", p=P)

        def load(sp, turn, slot, sources):
            if not (isinstance(turn, int) and turn == 0):
                sp.wait_ge(lo_ready, turn * RING + (slot + 1 - RING))
            for i, source in enumerate(sources):
                to = raw[:, slot, i * (CE // 2):(i + 1) * (CE // 2)]
                if len(source.shape) == 3:
                    to = to.rearrange("p (a c) -> p a c", a=2)
                sp.dma_start(to, source).then_inc(raw_landed[slot], 16)

        def round_hi(a, turn, slot):
            a.wait_ge(raw_landed[slot], turn * 32 + 32)
            if not (isinstance(turn, int) and turn == 0):
                a.wait_ge(chunks_done, turn * RING + (slot + 1 - RING))
            nc.scalar.activation(w_hi[:, slot, :], raw[:, slot, :], ACT.Copy).then_inc(hi_ready, 1)

        def take_lo(v, turn, slot):
            v.wait_ge(hi_ready, turn * RING + (slot + 1))
            v.tensor_tensor(w_lo[:, slot, :], raw[:, slot, :], w_hi[:, slot, :].bitcast(F32),
                                    ALU.subtract).then_inc(lo_ready, 1)

        SPLIT = {}

        def splits(eng, turn, slots=range(RING)):
            for s in slots:
                (round_hi if eng is SPLIT["act"] else take_lo)(eng, turn, s)

        def split_turns(eng, first, n):
            if n == 1:
                splits(eng, first)
            elif n > 1:
                with eng.Fori(0, n) as r:
                    splits(eng, r + first)

        def rows_chunk(pe, turn, slot, src, parts, first, last, bank_free=None, bank_done=None):
            pe.wait_ge(lo_ready, turn * RING + (slot + 1))
            for n, (bank, tok, products) in enumerate(parts):
                if first and bank_free is not None:
                    bank_free(n)
                for j, (k, col) in enumerate(products):
                    hi = src[:, k, tok * P:(tok + 1) * P]
                    lo = src[:, k, T + tok * P:T + (tok + 1) * P]
                    wh = w_hi[:, slot, col:col + BANK]
                    wl = w_lo[:, slot, col:col + BANK]
                    nc.tensor.matmul(ps[:, bank, :], hi, wh, start=(first and j == 0), stop=False)
                    nc.tensor.matmul(ps[:, bank, :], hi, wl, start=False, stop=False)
                    mm = nc.tensor.matmul(ps[:, bank, :], lo, wh, start=False,
                                          stop=(last and j == len(products) - 1))
                if last and n < len(parts) - 1:
                    mm.then_inc(bank_done, 1)
            mm.then_inc(chunks_done, 1)

        def halves(pe, name, src, kt, free, done, src_ready=None):
            with pe.Fori(0, 2) as h:
                for k in range(kt - RING):
                    turn = h * (kt // RING) + (TURN[name] + k // RING)
                    parts = [(tok * 2 + n, tok, [(k, n * BANK)]) for tok in range(TT) for n in range(2)]
                    if src_ready is not None and k % 2 == 0:
                        pe.wait_ge(src_ready[0], k // 2 + 1 + src_ready[1])
                    rows_chunk(pe, turn, k % RING, src, parts, k == 0, False,
                               lambda b: pe.wait_ge(free, h * (b + 1) + 1))
                end = range(kt - RING, kt)
                order = [(bank, k) for bank in (0, 1) for k in end[:-1]] + [(bank, end[-1]) for bank in (0, 1)]
                order += [(bank, end[0]) for bank in (2, 3)] + [(bank, k) for bank in (2, 3) for k in end[1:]]
                for bank, k in order:
                    tok, n, slot = bank // 2, bank % 2, k % RING
                    if bank == 0:
                        if src_ready is not None and k % 2 == 0:
                            pe.wait_ge(src_ready[0], k // 2 + 1 + src_ready[1])
                        pe.wait_ge(lo_ready, h * kt + (TURN[name] * RING + k + 1))
                    hi = src[:, k, tok * P:(tok + 1) * P]
                    lo = src[:, k, T + tok * P:T + (tok + 1) * P]
                    wh = w_hi[:, slot, n * BANK:(n + 1) * BANK]
                    wl = w_lo[:, slot, n * BANK:(n + 1) * BANK]
                    nc.tensor.matmul(ps[:, bank, :], hi, wh, start=False, stop=False)
                    nc.tensor.matmul(ps[:, bank, :], hi, wl, start=False, stop=False)
                    mm = nc.tensor.matmul(ps[:, bank, :], lo, wh, start=False, stop=(k == kt - 1))
                    if bank == 3:
                        mm.then_inc(chunks_done, 1)
                    elif k == kt - 1:
                        mm.then_inc(done, 1)

        def groups(pe, name, n_groups, before, start, cross=True, middle=None, gate_done=None):
            def group(pair, b, before=None):
                for j in range(KD // 2):
                    slot = j % RING
                    turn = pair * 4 + (TURN[name] + 2 * b + j // RING)
                    if j == 0:
                        start(pair * 2 + b, b)
                    if before is not None:
                        before(j)
                    if j == RING and middle is not None and not (before is not None and b == 0):
                        middle(pair * 2 + b, b)
                    pe.wait_ge(lo_ready, turn * RING + (slot + 1))
                    for m in ((0, 1, 2, 3) if cross else (2, 3, 0, 1)):
                        for kk in range(2):
                            k = 2 * j + kk
                            bank = 4 * b + m
                            col = (m // 2) * 512 + kk * 256 + (m % 2) * P
                            wh, wl = w_hi[:, slot, col:col + P], w_lo[:, slot, col:col + P]
                            if not cross:
                                nc.tensor.matmul(ps[:, bank, 0:T], wl, xT[:, k, 0:T], start=(k == 0), stop=False)
                                nc.tensor.matmul(ps[:, bank, 0:T], wh, xT[:, k, 0:T], start=False, stop=False)
                                mm = nc.tensor.matmul(ps[:, bank, 0:T], wh, xT[:, k, T:2 * T], start=False,
                                                      stop=(k == KD - 1))
                                if m == 3 and k == KD - 1:
                                    mm.then_inc(gate_done, 1)
                                continue

                            def low():
                                nc.tensor.matmul(ps[:, bank, 0:T], wl, xT[:, k, 0:T],
                                                 start=False, stop=False, skip_group_check=True)
                            if k > 0:
                                low()
                            mm = nc.tensor.matmul(ps[:, bank, :], wh, xT[:, k, :],
                                                  start=(k == 0), stop=(k == KD - 1), skip_group_check=True)
                            if k == 0:
                                low()
                    mm.then_inc(chunks_done, 1)
            group(0, 0, before)
            group(0, 1)
            with pe.Fori(1, n_groups // 2) as pair:
                for b in range(2):
                    group(pair, b)

        def group_loads(sp, name, n_groups):
            with sp.Fori(0, n_groups) as g:
                for j in range(KD // 2):
                    v = w_view[name]
                    load(sp, g * 2 + (TURN[name] + j // RING), j % RING,
                         [v[:, 2 * j:2 * j + 2, s, bass.ds(g * 256, 256)] for s in range(2)])

        def half_loads(sp, name, kt):
            with sp.Fori(0, 2) as h:
                for k in range(kt):
                    v = w_view[name]
                    load(sp, h * (kt // RING) + (TURN[name] + k // RING), k % RING,
                         [v[:, k, bass.ds(h * HALF + n * BANK, BANK)] for n in range(2)])

        def half_loads_k(sp, name, kt):
            with sp.Fori(0, 2) as h:
                with sp.Fori(0, kt // RING) as r:
                    for s in range(RING):
                        v = w_down[int(name[-1])]
                        rowsv = v[bass.ds(r * (RING * P) + s * P, P), bass.ds(h * HALF, HALF)]
                        load(sp, h * (kt // RING) + r + TURN[name], s,
                             [rowsv[:, n * BANK:(n + 1) * BANK] for n in range(2)])

        def load_rows(eng, n, name):
            eng.wait_ge(chunks_done, TURN[name] * RING)
            for i, v in enumerate((norm_g, norm_b)):
                eng.dma_start(rows[:, i, :], broadcast_rows(v[n // 2, n % 2:n % 2 + 1])
                              ).then_inc(rows_landed[n], 16)

        class Norm:
            def __init__(self, n):
                self.n = n
                self.bank_done = sem(f"bank_done{n}")
                self.summed = sem(f"summed{n}")
                self.stats = sem(f"stats{n}")
                self.small = sem(f"small{n}")
                self.std = sem(f"std{n}")
                self.centred = sem(f"centred{n}")
                self.turned = sem(f"turned{n}")
                self.affine_v, self.affine_a = sem(f"affine_v{n}"), sem(f"affine_a{n}")
                self.hi = sem(f"xT_hi{n}")
                self.lo = sem(f"xT_lo{n}")
        norms = [Norm(n) for n in range(4)]
        res = sem("residual")

        class Group:
            def __init__(self, n):
                self.free = sem(f"acc_free{n}")
                self.cross = sem(f"cross{n}")
                self.taps = sem(f"taps{n}")
                self.act = sem(f"gate_act{n}")
                self.gated = sem(f"gated{n}")
                self.hi = sem(f"hT_hi{n}")
                self.lo = sem(f"hT_lo{n}")
        ffn = [Group("_up0"), Group("_up1")]
        cin = Group("_in")
        glu_done, pads_made = sem("glu_done"), sem("pads_made")
        gate_products, glu_hi, glu_lo = sem("gate_products"), sem("glu_hi"), sem("glu_lo")
        first_hi, first_lo = sem("first_hi"), sem("first_lo")
        taps_split, diag_ready, last_diag_ready = sem("taps_split"), sem("diag_ready"), sem("last_diag_ready")
        pe_taps_done, last_tile_out = sem("pe_taps_done"), sem("last_tile_out")

        NT = 4 * FW

        def ffn_act(a, l, g, b, t0):
            s = ffn[l]
            turn = g * 2 + t0
            a.wait_ge(chunks_done, (turn + 2) * RING)
            for side in range(2):
                a.wait_ge(s.free, g * 2 + (side + 1 + 2))
                nc.scalar.activation(cross[:, side], ps[:, 4 * b + 2 * side:4 * b + 2 * side + 2, T:2 * T],
                                     ACT.Copy).then_inc(s.cross, 1)
            splits(a, turn + 2, [3])
            splits(a, turn + 3, [0])
            a.wait_ge(s.taps, (g + 1) * NT + 1)
            a.wait_ge(s.gated, g + 1)
            nc.scalar.activation(act[:], conv[:, 0], ACT.Silu).then_inc(s.act, 1)
            splits(a, turn + 3, [1])
            a.wait_ge(s.gated, g + 2)
            nc.scalar.activation(hT[:, bass.ds(g * 2, 2), 0:T], up[:, 0], ACT.Copy).then_inc(s.hi, 1)
            splits(a, turn + 3, [2, 3])
            splits(a, turn + 4, [0, 1, 2])

        def add_cross(v, s, g, b):
            for side in range(2):
                v.wait_ge(s.cross, g * 2 + (side + 1))
                nc.vector.tensor_tensor(up[:, side], cross[:, side],
                                        ps[:, 4 * b + 2 * side:4 * b + 2 * side + 2, 0:T], ALU.add
                                        ).then_inc(s.free, 1)

        def ffn_dve(v, l, g, b, t0):
            turn = g * 2 + t0
            s = ffn[l]
            v.wait_ge(s.hi, g + 1)
            v.wait_ge(s.lo, g + 1)
            v.wait_ge(s.taps, g * NT + 1)
            add_cross(v, s, g, b)
            splits(v, turn + 2, [3])
            tiles = [(side, m) for side in range(2) for m in range(2)]
            for j in range(FW):
                for n, (side, m) in enumerate(tiles):
                    tap = ffn_taps[:, l, FW - 1 - j, bass.ds(g * 2 + (side * KF + m), 1)]
                    if j == 0:
                        v.wait_ge(s.free, g * 2 + (side + 1 + 4))
                        if n == 0:
                            v.wait_ge(s.act, g + 1)
                            v.wait_ge(s.gated, g + 1)
                        nc.vector.tensor_scalar(conv[:, side, m], up[:, side, m], tap, None, ALU.mult
                                                ).then_inc(s.taps, 1)
                    else:
                        v.wait_ge(s.taps, g * NT + (4 * j - 2 + n))
                        nc.vector.scalar_tensor_tensor(
                            out=conv[:, side, m, j:T], in0=up[:, side, m, 0:T - j], scalar=tap,
                            in1=conv[:, side, m, j:T], op0=ALU.mult, op1=ALU.add).then_inc(s.taps, 1)
            splits(v, turn + 3, [0])
            v.wait_ge(s.act, g + 2)
            v.wait_ge(s.taps, (g + 1) * NT + 1)
            nc.vector.tensor_tensor(up[:, 0], act[:], conv[:, 1], ALU.mult).then_inc(s.gated, 1)
            splits(v, turn + 3, [1])
            v.wait_ge(s.gated, g + 2)
            v.wait_ge(s.hi, g + 2)
            h = hT[:, bass.ds(g * 2, 2), :]
            nc.vector.tensor_tensor(h[:, :, T:2 * T], up[:, 0], h[:, :, 0:T].bitcast(F32), ALU.subtract
                                    ).then_inc(s.lo, 1)
            splits(v, turn + 3, [2, 3])
            splits(v, turn + 4, [0, 1, 2])

        def cin_act(a, g, b):
            s = cin
            a.wait_ge(gate_products, g + 1)
            a.wait_ge(glu_done, g + 1)
            nc.scalar.activation(act[:], ps[:, 4 * b + 2:4 * b + 4, 0:T], ACT.Sigmoid).then_inc(s.act, 1)

        def cin_hi(a, g):
            a.wait_ge(glu_done, g + 2)
            a.wait_ge(glu_lo, g + 1)
            a.wait_ge(pe_taps_done, g + 2)
            nc.scalar.activation(glu_split[:, 0], glu[:, 1], ACT.Copy).then_inc(glu_hi, 1)

        def make_diag(a, to, tile, j, done):
            for half, taps in enumerate((conv_taps, taps_lo)):
                nc.scalar.activation(to[:, half], ident[:], ACT.Copy, scale=taps[:, tile, j]).then_inc(done, 1)

        def cin_diags(a, g, b, part):
            if part == 0:
                a.wait_ge(taps_split, 2)
                a.wait_ge(pe_taps_done, g + 1)
            for i in range(part * PE_TAPS // RING, (part + 1) * PE_TAPS // RING):
                j = DVE_TAPS + i
                make_diag(a, diag[:, b, i], bass.ds(g * 2 + 1, 1), slice(j, j + 1), diag_ready)

        def cin_last_diags(a, g, part, parts):
            if not isinstance(g, int):
                jobs = [(last_diag[:, bass.ds(g * EXTRA + i, 1)].squeeze(1), slice(KD - 1, KD),
                         bass.ds(g * EXTRA + i, 1)) for i in range(EXTRA)]
            else:
                jobs = [(last_diag[:, i], slice(KD - 1, KD), slice(i, i + 1))
                        for i in range(EXTRA * (KD // 2 - 2), DVE_TAPS)]
                jobs += [(last_diag[:, i], slice(KD - 2, KD - 1), slice(CW - LAST_TAPS + i, CW - LAST_TAPS + i + 1))
                         for i in range(DVE_TAPS, LAST_TAPS)]
            for job in jobs[part * len(jobs) // parts:(part + 1) * len(jobs) // parts]:
                make_diag(a, *job, last_diag_ready)

        STEPS = []
        for _j in range(CW):
            STEPS.append((0, _j))
            if _j < DVE_TAPS:
                STEPS.append((1, _j))
            if _j == 20:
                STEPS.append((1, None))
        NS = len(STEPS)
        SUM_STEP = STEPS.index((1, None))
        LAST_STEPS = [(0, j) for j in range(CW - FIRST_TAPS)] + [(0, None)]

        def cin_glu(v, g, b):
            s = cin
            v.wait_ge(chunks_done, (TURN["w_in"] + 2 + g * 2) * RING)
            v.wait_ge(s.act, g + 2)
            v.wait_ge(s.taps, g * NS + 1)
            v.wait_ge(glu_lo, g + 1)
            nc.vector.tensor_tensor(glu[:, :, CW - 1:], ps[:, 4 * b:4 * b + 2, 0:T], act[:], ALU.mult
                                    ).then_inc(glu_done, 1)

        def first_tile_hi(a):
            a.wait_ge(glu_done, KD // 2 + 1)
            nc.scalar.activation(first_split[:, 0], glu[:, 0], ACT.Copy).then_inc(first_hi, 1)

        def first_tile_lo(v):
            v.wait_ge(first_hi, 1)
            nc.vector.tensor_tensor(first_split[:, 1], glu[:, 0], first_split[:, 0].bitcast(F32), ALU.subtract
                                    ).then_inc(first_lo, 1)

        def cin_lo(v, g):
            v.wait_ge(glu_hi, g + 1)
            v.wait_ge(pe_taps_done, g + 2)
            nc.vector.tensor_tensor(glu_split[:, 1], glu[:, 1], glu_split[:, 0].bitcast(F32), ALU.subtract
                                    ).then_inc(glu_lo, 1)

        def cin_steps(v, g, bank, steps, between):
            s = cin
            before = {}
            v.wait_ge(glu_done, g + 2)
            for i, (m, j) in enumerate(steps):
                o = conv_out[:, bass.ds(g * 2 + m, 1), :]
                if m in before:
                    v.wait_ge(s.taps, g * NS + (before[m] + 2))
                if j is None:
                    v.wait_ge(pe_taps_done, g + 3)
                    step = nc.vector.tensor_tensor(o, o, ps[:, bank:bank + 1, 0:T], ALU.add)
                else:
                    tap, src = conv_taps[:, bass.ds(g * 2 + m, 1), j], glu[:, m:m + 1, j:j + T]
                    if j == 0:
                        step = nc.vector.tensor_scalar(o, src, tap, None, ALU.mult)
                    else:
                        step = nc.vector.scalar_tensor_tensor(out=o, in0=src, scalar=tap, in1=o, op0=ALU.mult,
                                                              op1=ALU.add)
                step.then_inc(s.taps, 1)
                before[m] = i
                between(i)

        def bank_complete(v, s, name, kt, h, b):
            if b < 3:
                v.wait_ge(s.bank_done, 3 * h + b + 1)
            else:
                v.wait_ge(chunks_done, TURN[name] * RING + kt * (h + 1))

        def add_bank(v, n, name, kt, h, b):
            s = norms[n]
            tok, c = b // 2, h * 2 + b % 2
            cols = x[:, tok, c * BANK:(c + 1) * BANK]
            bank_complete(v, s, name, kt, h, b)
            nc.vector.scalar_tensor_tensor(out=cols, in0=cols, scalar=ALPHA, in1=ps[:, b, :],
                                           op0=ALU.mult, op1=ALU.add).then_inc(s.summed, 1)

        def stat(v, s, h, b):
            tok, c = b // 2, h * 2 + b % 2
            v.wait_ge(s.summed, 4 * h + b + 2)
            nc.vector.bn_stats(stats[:, tok, c, :], x[:, tok, c * BANK:(c + 1) * BANK]).then_inc(s.stats, 1)

        def deviation(v, small, std_sem, toks, base, roots):
            count = base
            for tok in toks:
                nc.vector.bn_aggr(mv[:, tok, :], stats[:, tok]).then_inc(small, 1)
                count += 1
            t = slice(toks[0], toks[-1] + 1)
            v.wait_ge(small, count)
            nc.vector.tensor_scalar(var_eps[:, t], mv[:, t, 1], EPS, None, ALU.add).then_inc(small, 1)
            v.wait_ge(std_sem, roots + 1)
            nc.vector.reciprocal(rstd[:, 1, t], std[:, t]).then_inc(small, 1)
            v.wait_ge(small, count + 2)
            nc.vector.tensor_tensor(newton[:, 0, t], rstd[:, 1, t], rstd[:, 1, t], ALU.mult).then_inc(small, 1)
            v.wait_ge(small, count + 3)
            nc.vector.tensor_tensor(newton[:, 1, t], newton[:, 0, t], var_eps[:, t], ALU.mult).then_inc(small, 1)
            v.wait_ge(small, count + 4)
            nc.vector.tensor_scalar(newton[:, 2, t], newton[:, 1, t], -0.5, 1.5, ALU.mult, ALU.add
                                    ).then_inc(small, 1)
            v.wait_ge(small, count + 5)
            nc.vector.tensor_tensor(rstd[:, 0, t], rstd[:, 1, t], newton[:, 2, t], ALU.mult).then_inc(small, 1)
            v.wait_ge(small, count + 6)

        TOK_STEPS = 7

        def root(a, small, std_sem, toks, base):
            t = slice(toks[0], toks[-1] + 1)
            a.wait_ge(small, base + len(toks) + 1)
            nc.scalar.activation(std[:, t], var_eps[:, t], ACT.Sqrt).then_inc(std_sem, 1)

        def centre(v, n, tok, c):
            cols = x[:, tok, c * BANK:(c + 1) * BANK]
            nc.vector.tensor_scalar(cols, cols, mv[:, tok, 0:1], rstd[:, 0, tok:tok + 1],
                                    ALU.subtract, ALU.mult).then_inc(norms[n].centred, 1)

        CENTRED = (3, 4, 6, 8)

        def turn_pe(pe, n):
            s = norms[n]

            def job(j):
                pe.wait_ge(s.centred, CENTRED[j // 2])
                if j >= 4:
                    pe.wait_ge((s.affine_v, s.affine_a)[j % 2], 2 * ((j - 4) // 2) + 2)
                turn_job(pe, 4 + j % 4, j).then_inc(s.turned, 1)

            def before(c):
                for j in (range(4) if c == 0 else range(2 * c + 2, 2 * c + 4) if c < 3 else []):
                    job(j)
                pe.wait_ge(s.lo, c + 1)
            return before

        def turn_job(pe, bank, j):
            for kk in range(2):
                for tok in range(TT):
                    k = 2 * j + kk
                    mm = nc.tensor.transpose(ps[:, bank, kk * T + tok * P:kk * T + (tok + 1) * P],
                                             x[:, tok, k * P:(k + 1) * P], ident[:])
            return mm

        def affine(eng, n, j):
            s = norms[n]
            eng.wait_ge(s.turned, j + 1)
            if j >= 2:
                eng.wait_ge(s.hi, j - 1)
                eng.wait_ge(s.lo, j - 1)
            for kk in range(2):
                k = 2 * j + kk
                src = ps[:, 4 + j % 4, kk * T:(kk + 1) * T]
                gain, bias = norm_cols[:, n, k:k + 1], norm_cols[:, 4 + n, k:k + 1]
                if j % 2:
                    mm = nc.scalar.activation(turned[:, 1, kk], src, ACT.Identity, bias=bias, scale=gain)
                else:
                    mm = nc.vector.tensor_scalar(turned[:, 0, kk], src, gain, bias, ALU.mult, ALU.add)
                mm.then_inc((s.affine_v, s.affine_a)[j % 2], 1)

        def turn_dve(v, n, early):
            s = norms[n]

            def low(j):
                v.wait_ge(s.hi, j + 1)
                hi = xT[:, 2 * j:2 * j + 2, 0:T].bitcast(F32)
                nc.vector.tensor_tensor(xT[:, 2 * j:2 * j + 2, T:2 * T], turned[:, j % 2], hi,
                                        ALU.subtract).then_inc(s.lo, 1)

            affine(v, n, 0)
            for j in range(KD // 2):
                if j % 2 and j + 1 < KD // 2:
                    affine(v, n, j + 1)
                low(j)
                early(j)

        def turn_act(a, n, early):
            s = norms[n]
            for j in range(KD // 2):
                if j % 2 == 0:
                    affine(a, n, j + 1)
                a.wait_ge((s.affine_v, s.affine_a)[j % 2], 2 * (j // 2) + 2)
                nc.scalar.activation(xT[:, 2 * j:2 * j + 2, 0:T], turned[:, j % 2], ACT.Copy).then_inc(s.hi, 1)
                early(j)

        def residual_piece(v, n, c):
            if c == 0:
                v.wait_ge(rows_landed[n], 32)
            for tok in range(TT):
                cols = x[:, tok, c * BANK:(c + 1) * BANK]
                nc.vector.tensor_tensor(cols, cols, rows[:, 0, c * BANK:(c + 1) * BANK], ALU.mult
                                        ).then_inc(res, 1)
            for tok in range(TT):
                cols = x[:, tok, c * BANK:(c + 1) * BANK]
                v.wait_ge(res, n * 16 + 4 * c + tok + 1)
                nc.vector.tensor_tensor(cols, cols, rows[:, 1, c * BANK:(c + 1) * BANK], ALU.add
                                        ).then_inc(res, 1)

        def half_phase(eng, name, kt, after_half, update=None, done=RING):
            n = kt // RING
            for h in range(2):
                first = TURN[name] + h * n
                at = done if h == 0 else RING
                turn = first + at // RING
                if at % RING:
                    splits(eng, turn, range(at % RING, RING))
                    turn += 1
                if update is not None and h == 0:
                    if done == RING:
                        splits(eng, turn)
                        turn += 1
                    for s in range(RING):
                        update(s)
                        splits(eng, turn, [s])
                    turn += 1
                split_turns(eng, turn, first + n - turn)
                after_half(h, first + n)

        k_tok_done, rotated, qk_turned, qk_ready = sem("k_tok_done"), sem("rotated"), sem("qk_turned"), sem("qk_ready")
        rot_step, copied, q_done = sem("rot_step"), sem("copied"), sem("q_done")
        sc_done, sc_masked, mx_step, neg_max = sem("sc_done"), sem("sc_masked"), sem("mx_step"), sem("neg_max")
        exp_done, den_step, norm_done = sem("exp_done"), sem("den_step"), sem("norm_done")
        pT_turned, pT_ready, o_done, o_hi, o_lo = (sem("pT_turned"), sem("pT_ready"), sem("o_done"), sem("o_hi"),
                                                   sem("o_lo"))
        UNITS = [(n, t) for n in range(NKV) for t in range(TT)]

        def width(t):
            return (t + 1) * P

        def psum_scores(u):
            t = UNITS[u][1]
            b = 2 * (u % 2)
            v = ps[:, b:b + 1 + t, :]
            return v.rearrange("p b (g k) -> p (b g) k", k=width(t))

        def rotate(v, view, tok, i):
            h = view.shape[1]
            c = rope_sb[:, tok, 0:ROT].unsqueeze(1).broadcast_to([P, h, ROT])
            s = rope_sb[:, tok, ROT:2 * ROT].unsqueeze(1).broadcast_to([P, h, ROT])
            v.wait_ge(copied, i + 1)
            if i >= 1:
                v.wait_ge(rotated, i)
            nc.vector.tensor_tensor(rot[:, 0, 0:h], view[:, :, 0:ROT], c, ALU.mult).then_inc(rot_step, 1)
            nc.vector.tensor_tensor(rot[:, 1, 0:h, 0:RH], view[:, :, RH:ROT], s[:, :, 0:RH], ALU.mult
                                    ).then_inc(rot_step, 1)
            nc.vector.tensor_tensor(rot[:, 1, 0:h, RH:ROT], view[:, :, 0:RH], s[:, :, RH:ROT], ALU.mult
                                    ).then_inc(rot_step, 1)
            v.wait_ge(rot_step, 3 * (i + 1))
            nc.vector.tensor_tensor(view[:, :, 0:ROT], rot[:, 0, 0:h], rot[:, 1, 0:h], ALU.add
                                    ).then_inc(rotated, 1)

        def q_view(tok, i):
            return q_tok[:, tok, i].rearrange("p g e d -> p (g e) d")

        kv_bank_done, q_bank_done, q_free = sem("kv_bank_done"), sem("q_bank_done"), sem("q_free")
        v_copied = sem("v_copied")

        c_turned, c_stats, c_small, c_std, c_shift = (sem("c_turned"), sem("c_stats"), sem("c_small"), sem("c_std"),
                                                      sem("c_shift"))
        c_bcast, c_scaled, c_norm, c_silu, s_hi, s_lo = (sem("c_bcast"), sem("c_scaled"), sem("c_norm"),
                                                         sem("c_silu"), sem("s_hi"), sem("s_lo"))

        C_TURNED = [(0, 0, 1), (0, 1, 2), (0, 2, 3), (1, 0, 5), (1, 1, 6), (1, 2, 7), (0, 3, 0), (1, 3, 1)]

        block = ctx.enter_context(nc.Block())

        @block.sync
        def _(sp):
            def kv_load(name, j):
                load(sp, TURN[name] + j // RING, j % RING, [w_view[name][:, 2 * j + kk, :] for kk in range(2)])
            for i in range(4):
                for tok in range(TT):
                    sp.dma_start(x[:, tok, i * BANK:(i + 1) * BANK],
                                 x_in[0, tok * P:(tok + 1) * P, i * BANK:(i + 1) * BANK]
                                 ).then_inc(x_landed[i], 16)
                kv_load("wk", i)
            for j in range(RING, KD // 2):
                kv_load("wk", j)
            for j in range(KD // 2):
                kv_load("wv", j)
            half_loads(sp, "wq", KD)
            half_loads(sp, "wo", KD)
            group_loads(sp, "up0", KF // 2)
            half_loads_k(sp, "down0", KF)
            group_loads(sp, "w_in", KD // 2)
            half_loads(sp, "w_out", KD)
            group_loads(sp, "up1", KF // 2)
            half_loads_k(sp, "down1", KF)
            for c in range(4):
                for tok in range(TT):
                    sp.wait_ge((first_out, second_out)[tok], c + 1)
                    sp.dma_start(out[0, tok * P:(tok + 1) * P, c * BANK:(c + 1) * BANK],
                                 x[:, tok, c * BANK:(c + 1) * BANK]).then_inc(stored, 16)
            sp.wait_ge(stored, 16 * 4 * TT)

        @block.gpsimd
        def _(pool):
            nc.gpsimd.memset(ident[:], 1.0).then_inc(ident_made, 1)
            pool.wait_ge(ident_made, 1)
            nc.gpsimd.affine_select(out=ident[:], in_=ident[:], compare_op=ALU.is_equal, fill=0.0, base=0,
                                    pattern=[[-1, P]], channel_multiplier=1).then_inc(ident_made, 1)
            for i, v in enumerate((norm_g, norm_b)):
                pool.dma_start(norm_rows[64 * i:64 * (i + 1), :], v.rearrange("l s (t p) -> (l s t) p", p=P)
                               ).then_inc(vectors_landed, 16)
            for i, v in enumerate((conv_g, conv_b)):
                pool.dma_start(convn_rows[KD * i:KD * (i + 1), :], v[0].rearrange("(t p) -> t p", p=P)
                               ).then_inc(vectors_landed, 16)
            for l in range(DEPTH):
                pool.dma_start(tap_rows[:, l], ffn_dw[l].rearrange("j (t p) -> t j p", p=P)
                               ).then_inc(vectors_landed, 16)
            pool.dma_start(dw_rows[:], conv_dw[0]).then_inc(vectors_landed, 16)
            pool.dma_start(rope_sb[:], rope.rearrange("(t p) c -> p t c", p=P)).then_inc(rope_landed, 16)
            pool.dma_start(sink[:], broadcast_rows(sinks)).then_inc(sink_landed, 16)
            def first_turn(name):
                pool.wait_ge(lo_ready, TURN[name] * RING)
                for slot in range(RING):
                    take_lo(pool, TURN[name], slot)

            first_turn("up0")
            load_rows(pool, 0, "down0")
            first_turn("w_in")
            with pool.Fori(0, TURN["w_out"] - TURN["w_in"] + 1) as r:
                for slot in range(RING):
                    take_lo(pool, r + TURN["w_in"] + 1, slot)
            first_turn("up1")
            load_rows(pool, 2, "down1")
            pool.wait_ge(res, 3 * 16)
            for i, v in enumerate((norm_g, norm_b)):
                pool.dma_start(rows[:, i, :], broadcast_rows(v[1, 1:2])).then_inc(rows_landed[3], 16)
            pool.wait_ge(rows_landed[3], 32)
            for c in range(4):
                cols = slice(c * BANK, (c + 1) * BANK)
                pool.wait_ge(first_centred, 2 * (c + 1))
                nc.gpsimd.tensor_tensor(x[:, 0, cols], x[:, 0, cols], rows[:, 0, cols], ALU.mult
                                        ).then_inc(first_gain, 1)
                pool.wait_ge(first_gain, c + 1)
                nc.gpsimd.tensor_tensor(x[:, 0, cols], x[:, 0, cols], rows[:, 1, cols], ALU.add
                                        ).then_inc(first_out, 1)

        @block.scalar
        def _(a):
            SPLIT["act"] = a
            for s in (ffn[0].act, ffn[0].hi, ffn[1].act, ffn[1].hi, cin.act, pe_taps_done,
                      pe_taps_done):
                a.sem_inc(s, 1)
            for j in range(KD // 2):
                a.wait_ge(x_turned, j + 1)
                nc.scalar.activation(xT[:, 2 * j:2 * j + 2, 0:T],
                                     ps[:, 4 + j % 4, :].rearrange("p (k t) -> p k t", k=2), ACT.Copy
                                     ).then_inc(x_hi, 1)
                if j % 2:
                    round_hi(a, 0, j // 2)
            for t in range(1, TURN["wq"] + 1):
                if t == TURN["wq"]:
                    splits(a, t, range(RING - 1))
                    for tok in range(TT):
                        if tok == 0:
                            a.wait_ge(kv_bank_done, 2)
                        else:
                            a.wait_ge(chunks_done, TURN["wq"] * RING)
                        nc.scalar.activation(v_tok[:, tok], ps[:, 2 + tok, :], ACT.Copy).then_inc(v_copied, 1)
                    splits(a, t, [RING - 1])
                else:
                    splits(a, t)
                    if t == TURN["wv"]:
                        for tok in range(TT):
                            if tok == 0:
                                a.wait_ge(kv_bank_done, 1)
                            else:
                                a.wait_ge(chunks_done, TURN["wv"] * RING)
                            nc.scalar.activation(k_tok[:, tok], ps[:, tok, :], ACT.Copy).then_inc(copied, 1)

            def q_out(h, turn):
                splits(a, turn, range(RING - 1))
                for b in range(4):
                    tok, i = b // 2, 2 * h + b % 2
                    if b < 3:
                        a.wait_ge(q_bank_done, 3 * h + b + 1)
                    else:
                        a.wait_ge(chunks_done, TURN["wq"] * RING + KD * (h + 1))
                    nc.scalar.activation(q_tok[:, tok, i].rearrange("p g e d -> p e g d"),
                                         ps[:, b, :].rearrange("p (e g d) -> p e g d", e=2, g=GR),
                                         ACT.Copy).then_inc(copied, 1)
                splits(a, turn, [RING - 1])

            half_phase(a, "wq", KD, q_out)
            for i in range(10):
                a.wait_ge(qk_turned, i + 1)
                if i < 2:
                    to = kT[:, :, i * P:(i + 1) * P]
                else:
                    h, b = (i - 2) // 4, (i - 2) % 4
                    tok, kv = b // 2, 2 * h + b % 2
                    to = qT[:, kv * GR:(kv + 1) * GR, tok * P:(tok + 1) * P]
                nc.scalar.activation(to, ps[:, 4 + i % 4, :].rearrange("p (g t) -> p g t", g=4), ACT.Copy
                                     ).then_inc(qk_ready, 1)

            def exps(u):
                t = UNITS[u][1]
                p = probs[:, u % AB, :, 0:width(t)]
                sm = smalls[:, u % AB]
                a.wait_ge(neg_max, u + 1)
                for g in range(GR):
                    nc.scalar.activation(p[:, g], p[:, g], ACT.Exp, bias=sm[:, 2, g:g + 1],
                                         accum_out=sm[:, 4, g:g + 1]).then_inc(exp_done, 1)
                nc.scalar.activation(sm[:, 5], sm[:, 3], ACT.Exp).then_inc(exp_done, 1)

            def turned_out(u):
                t = UNITS[u][1]
                a.wait_ge(pT_turned, u + 1)
                if u >= AB:
                    a.wait_ge(o_done, u + 1 - AB)
                b = (t + 1) * GR
                nc.scalar.activation(probsT[:, u % AB, 0:b, :],
                                     ps[:, 4:5 + t, :].rearrange("p b (g q) -> p (b g) q", q=P), ACT.Copy
                                     ).then_inc(pT_ready, 1)

            def heads_out(u):
                n, t = UNITS[u]
                a.wait_ge(o_done, u + 1)
                nc.scalar.activation(hT[:, 2 * n:2 * n + 2, t * P:(t + 1) * P],
                                     ps[:, 6 + u % 2, 0:2 * P].rearrange("p (j q) -> p j q", j=2), ACT.Copy
                                     ).then_inc(o_hi, 1)

            exps(0)
            for u in range(len(UNITS) + 2):
                if u + 1 < len(UNITS):
                    exps(u + 1)
                if u < len(UNITS):
                    turned_out(u)
                if u >= 2:
                    heads_out(u - 2)

            def early_hi(turn):
                return lambda j: splits(a, turn + 1, [j - 4]) if 4 <= j < 3 + RING else None

            def norm_act(n):
                def after(h, turn):
                    s = norms[n]
                    if h == 0:
                        splits(a, turn)
                        nc.scalar.preload_act_table(ACT.Sqrt)
                        return
                    root(a, s.small, s.std, [0], 0)
                    if n < 3:
                        splits(a, turn, range(RING - 1))
                    if n == 3:
                        a.wait_ge(first_known, 1)
                        for c in range(4):
                            cols = x[:, 0, c * BANK:(c + 1) * BANK]
                            nc.scalar.activation(cols, cols, ACT.Identity, bias=shift[:, 0:1]
                                                 ).then_inc(first_centred, 1)
                            a.wait_ge(first_centred, 2 * c + 1)
                            nc.scalar.activation(cols, cols, ACT.Copy, scale=rstd[:, 0, 0:1]
                                                 ).then_inc(first_centred, 1)
                            if c == 1:
                                root(a, s.small, s.std, [1], TOK_STEPS)
                        return
                    root(a, s.small, s.std, [1], TOK_STEPS)
                    if n < 3:
                        nc.scalar.preload_act_table(ACT.Sigmoid if n == 1 else ACT.Silu)
                        splits(a, turn, [RING - 1])
                        turn_act(a, n, early_hi(turn))
                return after

            half_phase(a, "wo", KD, norm_act(0))

            def ffn_phase(l):
                t0 = TURN[f"up{l}"]
                splits(a, t0 + 1, [RING - 1])
                splits(a, t0 + 2, range(RING - 1))
                with a.Fori(0, KF // 4) as pair:
                    for b in range(2):
                        ffn_act(a, l, pair * 2 + b, b, t0)

            ffn_phase(0)
            half_phase(a, "down0", KF, norm_act(1), done=11)
            t0 = TURN["w_in"]
            a.wait_ge(chunks_done, t0 * RING)
            nc.scalar.activation(taps_hi[:], conv_taps[:], ACT.Copy).then_inc(taps_split, 1)

            def cin_group(g, b):
                for c in range(RING):
                    splits(a, g * 2 + (t0 + 1 + (c + 3) // RING), [(c + 3) % RING])
                    cin_diags(a, g, b, c)
                cin_act(a, g, b)
                if isinstance(g, int) and b == 1:
                    nc.scalar.preload_act_table(ACT.Sqrt)
                    first_tile_hi(a)
                    cin_hi(a, g)
                    splits(a, g * 2 + (t0 + 2), [RING - 1])
                    load_rows(a, 1, "w_out")
                    return
                splits(a, g * 2 + (t0 + 2), [RING - 1])
                for c in range(RING - 1):
                    splits(a, g * 2 + (t0 + 3), [c])
                    if c == 0:
                        cin_hi(a, g)
                    cin_last_diags(a, g, c, RING - 1)
            with a.Fori(0, KD // 4 - 1) as pair:
                for b in range(2):
                    cin_group(pair * 2 + b, b)
            for b in range(2):
                cin_group(KD // 2 - 2 + b, b)
            a.wait_ge(pe_taps_done, 3 + KD // 2)
            nc.scalar.activation(conv_out[:, KD - 1], ps[:, 4, 0:T], ACT.Copy).then_inc(last_tile_out, 1)
            root(a, c_small, c_std, range(TT), 0)
            for j in range(KD // 2):
                if 3 <= j < 3 + RING:
                    splits(a, TURN["w_out"] + 1, [j - 3])
                a.wait_ge(c_norm, j + 1)
                for kk in range(2):
                    k = 2 * j + kk
                    if j >= 1:
                        a.wait_ge(s_lo, j)
                    nc.scalar.activation(silu_out[:, kk], conv_out[:, k], ACT.Silu, bias=conv_cols[:, 1, k:k + 1],
                                         scale=conv_cols[:, 0, k:k + 1]).then_inc(c_silu, 1)
                a.wait_ge(c_silu, 2 * j + 2)
                nc.scalar.activation(hT[:, 2 * j:2 * j + 2, 0:T], silu_out[:], ACT.Copy).then_inc(s_hi, 1)
            half_phase(a, "w_out", KD, norm_act(2), done=2 * RING)
            ffn_phase(1)

            half_phase(a, "down1", KF, norm_act(3), done=11)

        @block.vector
        def _(v):
            for s in (ffn[0].taps, ffn[0].gated, ffn[0].lo, ffn[1].taps, ffn[1].gated, ffn[1].lo, cin.taps,
                      glu_done, glu_lo, norms[0].summed, norms[1].summed, norms[2].summed, norms[3].summed):
                v.sem_inc(s, 1)
            nc.vector.memset(mask[:], MASKED).then_inc(mask_made, 1)
            v.wait_ge(mask_made, 1)
            for part, lo, hi in ((0, 0, CHUNK), (64, 0, P), (0, P + CHUNK, P + 3 * CHUNK), (64, 2 * P, 2 * P + P)):
                nc.vector.memset(mask[part:part + CHUNK, lo:hi], 0.0).then_inc(mask_made, 1)
            for j in range(KD // 2):
                v.wait_ge(x_hi, j + 1)
                nc.vector.tensor_tensor(xT[:, 2 * j:2 * j + 2, T:2 * T],
                                        ps[:, 4 + j % 4, :].rearrange("p (k t) -> p k t", k=2),
                                        xT[:, 2 * j:2 * j + 2, 0:T].bitcast(F32), ALU.subtract).then_inc(x_lo, 1)
                if j % 2:
                    take_lo(v, 0, j // 2)
            for t in range(1, TURN["wq"] + 1):
                splits(v, t, range(RING - 1))
                if t == TURN["wv"] + 1:
                    v.wait_ge(rope_landed, 16)
                    for tok in range(TT):
                        rotate(v, k_tok[:, tok].rearrange("p (h d) -> p h d", d=HD), tok, tok)
                splits(v, t, [RING - 1])

            v.wait_ge(vectors_turned, 4)
            nc.vector.tensor_copy(norm_cols[:].rearrange("p a t -> p (a t)"), ps[:, 4, 0:P]).then_inc(vectors_ready, 1)
            nc.vector.tensor_copy(conv_cols[:].rearrange("p a t -> p (a t)"), ps[:, 4, P:P + 2 * KD]
                                  ).then_inc(vectors_ready, 1)
            for l in range(DEPTH):
                nc.vector.tensor_copy(ffn_taps[:, l].rearrange("p j t -> p (j t)"), ps[:, 5 + l, 0:FW * 2 * KF]
                                      ).then_inc(vectors_ready, 1)
            nc.vector.tensor_copy(conv_taps[:].rearrange("p t j -> p (t j)"), ps[:, 7, 0:KD * CW]
                                  ).then_inc(vectors_ready, 1)

            def q_rot(h, turn):
                splits(v, turn, range(RING - 1))
                for b in range(4):
                    tok, i = b // 2, 2 * h + b % 2
                    rotate(v, q_view(tok, i), tok, 2 + 4 * h + b)
                    if b == 1:
                        splits(v, turn, [RING - 1])

            half_phase(v, "wq", KD, q_rot)

            def masked(u):
                n, t = UNITS[u]
                w = width(t)
                sm = smalls[:, u % AB]
                sc = probs[:, u % AB, :, 0:w]
                v.wait_ge(sc_done, u + 1)
                if u >= AB:
                    v.wait_ge(pT_turned, u + 1 - AB)
                    v.wait_ge(norm_done, GR * (u + 1 - AB))
                m = mask[:, t * P:t * P + w].unsqueeze(1).broadcast_to([P, GR, w])
                nc.vector.scalar_tensor_tensor(out=sc, in0=psum_scores(u), scalar=SCALE,
                                               in1=m, op0=ALU.mult, op1=ALU.add).then_inc(sc_masked, 1)
                v.wait_ge(sc_masked, u + 1)
                nc.vector.tensor_reduce(sm[:, 0], sc, AX.X, ALU.max).then_inc(mx_step, 1)
                v.wait_ge(mx_step, 3 * u + 1)
                nc.vector.tensor_tensor(sm[:, 1], sm[:, 0], sink[:, n * GR:(n + 1) * GR], ALU.max
                                        ).then_inc(mx_step, 1)
                v.wait_ge(mx_step, 3 * u + 2)
                nc.vector.tensor_tensor(sm[:, 3], sink[:, n * GR:(n + 1) * GR], sm[:, 1], ALU.subtract
                                        ).then_inc(mx_step, 1)
                v.wait_ge(mx_step, 3 * u + 3)
                nc.vector.tensor_scalar(sm[:, 2], sm[:, 1], -1.0, None, ALU.mult).then_inc(neg_max, 1)

            def normalise(u):
                n, t = UNITS[u]
                sm = smalls[:, u % AB]
                v.wait_ge(exp_done, 5 * (u + 1))
                nc.vector.tensor_tensor(sm[:, 6], sm[:, 4], sm[:, 5], ALU.add).then_inc(den_step, 1)
                v.wait_ge(den_step, 2 * u + 1)
                nc.vector.reciprocal(sm[:, 7], sm[:, 6]).then_inc(den_step, 1)
                v.wait_ge(den_step, 2 * u + 2)
                for g in range(GR):
                    p = probs[:, u % AB, g, 0:width(t)]
                    nc.vector.tensor_scalar(p, p, sm[:, 7, g:g + 1], None, ALU.mult).then_inc(norm_done, 1)

            def heads_low(u):
                n, t = UNITS[u]
                v.wait_ge(o_hi, u + 1)
                nc.vector.tensor_tensor(hT[:, 2 * n:2 * n + 2, T + t * P:T + (t + 1) * P],
                                        ps[:, 6 + u % 2, 0:2 * P].rearrange("p (j q) -> p j q", j=2),
                                        hT[:, 2 * n:2 * n + 2, t * P:(t + 1) * P].bitcast(F32), ALU.subtract
                                        ).then_inc(o_lo, 1)

            v.wait_ge(sink_landed, 16)
            v.wait_ge(mask_made, 5)
            masked(0)
            masked(1)
            for u in range(len(UNITS) + 3):
                if u < len(UNITS):
                    normalise(u)
                if u + 2 < len(UNITS):
                    masked(u + 2)
                if u >= 3:
                    heads_low(u - 3)

            def norm_dve(n, name, kt, free=None):
                s = norms[n]

                def add(h, b):
                    add_bank(v, n, name, kt, h, b)

                def early_lo(turn):
                    def early(j):
                        if 4 <= j < 3 + RING:
                            if j == 4:
                                v.wait_ge(lo_ready, (turn + 1) * RING)
                            splits(v, turn + 1, [j - 4])
                    return early

                def after(h, turn):
                    if h == 0:
                        add(h, 0)
                        add(h, 1)
                        stat(v, s, h, 0)
                        stat(v, s, h, 1)
                        splits(v, turn, [0])
                        add(h, 2)
                        splits(v, turn, [1])
                        add(h, 3)
                        splits(v, turn, [2])
                        stat(v, s, h, 2)
                        stat(v, s, h, 3)
                        splits(v, turn, [3])
                        return
                    for b in (0, 1):
                        add(h, b)
                        stat(v, s, h, b)
                    v.wait_ge(s.stats, 6)
                    deviation(v, s.small, s.std, [0], 0, 0)
                    if n == 3:
                        nc.vector.tensor_scalar(shift[:, 0:1], mv[:, 0, 0:1], -1.0, None, ALU.mult
                                                ).then_inc(first_known, 1)
                    else:
                        centre(v, n, 0, 0)
                        centre(v, n, 0, 1)
                    add(h, 2)
                    stat(v, s, h, 2)
                    add(h, 3)
                    stat(v, s, h, 3)
                    if n < 3:
                        v.wait_ge(s.summed, 9)
                        v.sem_inc(free, 2)
                    v.wait_ge(s.stats, 8)
                    deviation(v, s.small, s.std, [1], TOK_STEPS, 1)
                    if n == 3:
                        return
                    for tok, c in ((1, 0), (1, 1), (0, 2), (1, 2), (0, 3), (1, 3)):
                        centre(v, n, tok, c)
                    if n < 3:
                        turn_dve(v, n, early_lo(turn) if n != 1 else lambda j: None)
                        v.wait_ge(s.affine_a, KD // 2)
                        v.wait_ge(s.affine_v, KD // 2)
                        v.sem_inc(free, 2)
                return after

            half_phase(v, "wo", KD, norm_dve(0, "wo", KD, ffn[0].free))

            def ffn_phase(l):
                t0 = TURN[f"up{l}"]
                splits(v, t0 + 1, [RING - 1])
                splits(v, t0 + 2, range(RING - 1))
                with v.Fori(0, KF // 4) as pair:
                    for b in range(2):
                        ffn_dve(v, l, pair * 2 + b, b, t0)

            ffn_phase(0)
            half_phase(v, "down0", KF, norm_dve(1, "down0", KF, cin.free),
                       update=lambda c: residual_piece(v, 0, c), done=11)
            nc.vector.memset(glu[:, :, 0:CW - 1], 0.0).then_inc(pads_made, 1)
            v.wait_ge(pads_made, 1)
            v.wait_ge(taps_split, 1)
            nc.vector.tensor_tensor(taps_lo[:], conv_taps[:], taps_hi[:].bitcast(F32), ALU.subtract
                                    ).then_inc(taps_split, 1)

            def cin_group(g, b):
                cin_glu(v, g, b)
                cin_steps(v, g, 4 * b, STEPS, lambda i: cin_lo(v, g) if i == 5 else None)
            with v.Fori(0, KD // 4 - 1) as pair:
                for b in range(2):
                    cin_group(pair * 2 + b, b)
            cin_group(KD // 2 - 2, 0)

            def c_stat(i):
                tok, c, bank = C_TURNED[i]
                v.wait_ge(c_turned, i + 1)
                nc.vector.bn_stats(stats[:, tok, c, :], ps[:, bank, :]).then_inc(c_stats, 1)

            def last_between(i):
                if i == 1:
                    first_tile_lo(v)
                if i == 3:
                    cin_lo(v, KD // 2 - 1)
                if i >= 5 and i % 3 == 2 and (i - 5) // 3 < 6:
                    c_stat((i - 5) // 3)
            cin_glu(v, KD // 2 - 1, 1)
            cin_steps(v, KD // 2 - 1, 0, LAST_STEPS, last_between)
            c_stat(6)
            c_stat(7)
            v.wait_ge(c_stats, 8)
            deviation(v, c_small, c_std, range(TT), 0, 0)
            nc.vector.tensor_tensor(newton[:, 0], mv[:, :, 0], rstd[:, 0], ALU.mult).then_inc(c_small, 1)
            v.wait_ge(c_small, 9)
            nc.vector.tensor_scalar(shift[:], newton[:, 0], -1.0, None, ALU.mult).then_inc(c_shift, 1)
            v.wait_ge(c_bcast, 1)

            def c_step(j):
                o = conv_out[:, 2 * j:2 * j + 2]
                nc.vector.tensor_tensor(o, o, ps[:, 4, 0:T].unsqueeze(1).broadcast_to([P, 2, T]), ALU.mult
                                        ).then_inc(c_scaled, 1)
                v.wait_ge(c_scaled, j + 1)
                nc.vector.tensor_tensor(o, o, ps[:, 4, T:2 * T].unsqueeze(1).broadcast_to([P, 2, T]), ALU.add
                                        ).then_inc(c_norm, 1)
            c_step(0)
            for j in range(KD // 2):
                if j + 1 < KD // 2:
                    c_step(j + 1)
                v.wait_ge(s_hi, j + 1)
                nc.vector.tensor_tensor(hT[:, 2 * j:2 * j + 2, T:2 * T], silu_out[:],
                                        hT[:, 2 * j:2 * j + 2, 0:T].bitcast(F32), ALU.subtract).then_inc(s_lo, 1)
            v.wait_ge(lo_ready, (TURN["w_out"] + 2) * RING)
            half_phase(v, "w_out", KD, norm_dve(2, "w_out", KD, ffn[1].free),
                       update=lambda c: residual_piece(v, 1, c), done=2 * RING)
            ffn_phase(1)
            def finish(c):
                cols = slice(c * BANK, (c + 1) * BANK)
                v.wait_ge(res, 3 * 16 + c + 1)
                nc.vector.scalar_tensor_tensor(out=x[:, 1, cols], in0=x[:, 1, cols], scalar=rstd[:, 0, 1:2],
                                               in1=rows[:, 1, cols], op0=ALU.mult, op1=ALU.add
                                               ).then_inc(second_out, 1)
            half_phase(v, "down1", KF, norm_dve(3, "down1", KF), update=lambda c: residual_piece(v, 2, c),
                       done=11)
            v.wait_ge(rows_landed[3], 32)
            for c in range(4):
                cols = slice(c * BANK, (c + 1) * BANK)
                nc.vector.scalar_tensor_tensor(out=x[:, 1, cols], in0=x[:, 1, cols], scalar=mv[:, 1, 0:1],
                                               in1=rows[:, 0, cols], op0=ALU.subtract, op1=ALU.mult
                                               ).then_inc(res, 1)
                if c > 0:
                    finish(c - 1)
            finish(3)

        @block.tensor
        def _(pe):
            pe.wait_ge(ident_made, 2)

            def turn_x(quarter):
                pe.wait_ge(x_landed[quarter], 32)
                for j in (2 * quarter, 2 * quarter + 1):
                    if j >= 4:
                        pe.wait_ge(x_lo, j - 3)
                    turn_job(pe, 4 + j % 4, j).then_inc(x_turned, 1)
            turn_x(0)
            for i, name in enumerate(("wk", "wv")):
                for j in range(KD // 2):
                    if i == 0:
                        if j < 3:
                            turn_x(j + 1)
                        pe.wait_ge(x_lo, j + 1)
                    parts = [(2 * i + tok, tok, [(2 * j, 0), (2 * j + 1, BANK)]) for tok in range(TT)]
                    rows_chunk(pe, TURN[name] + j // RING, j % RING, xT, parts, j == 0, j == KD // 2 - 1,
                               None, kv_bank_done)
            pe.wait_ge(vectors_landed, 16 * 7)
            nc.tensor.transpose(ps[:, 4, 0:P], norm_rows[:], ident[:])
            nc.tensor.transpose(ps[:, 4, P:P + 2 * KD], convn_rows[:], ident[0:2 * KD, 0:2 * KD]
                                ).then_inc(vectors_turned, 1)
            for l in range(DEPTH):
                for j in range(FW):
                    mm = nc.tensor.transpose(ps[:, 5 + l, j * 2 * KF:(j + 1) * 2 * KF], tap_rows[:, l, j, :],
                                             ident[0:2 * KF, 0:2 * KF])
                mm.then_inc(vectors_turned, 1)
            for t in range(KD):
                mm = nc.tensor.transpose(ps[:, 7, t * CW:(t + 1) * CW], dw_rows[:, t * P:(t + 1) * P],
                                         ident[0:CW, 0:CW])
            mm.then_inc(vectors_turned, 1)
            pe.wait_ge(copied, 2)
            pe.wait_ge(v_copied, 2)
            with pe.Fori(0, 2) as h:
                for k in range(KD):
                    turn = h * (KD // RING) + (TURN["wq"] + k // RING)
                    parts = [(tok * 2 + n, tok, [(k, n * BANK)]) for tok in range(TT) for n in range(2)]
                    rows_chunk(pe, turn, k % RING, xT, parts, k == 0, k == KD - 1,
                               lambda b: pe.wait_ge(copied, h * (b + 1) + 2), q_bank_done)
            pe.wait_ge(vectors_ready, 5)
            for i in range(10):
                if i >= 4:
                    pe.wait_ge(qk_ready, i - 3)
                pe.wait_ge(rotated, i + 1)
                for j in range(4):
                    if i < 2:
                        src = k_tok[:, i, j * P:(j + 1) * P]
                    else:
                        h, b = (i - 2) // 4, (i - 2) % 4
                        tok, kv = b // 2, 2 * h + b % 2
                        src = q_tok[:, tok, kv, j].rearrange("p e d -> p (e d)")
                    mm = nc.tensor.transpose(ps[:, 4 + i % 4, j * P:(j + 1) * P], src, ident[:])
                mm.then_inc(qk_turned, 1)
            pe.wait_ge(qk_ready, 10)

            def score(u):
                n, t = UNITS[u]
                e, i = n % 2, n // 2
                if u >= 2:
                    pe.wait_ge(sc_masked, u - 1)
                w = width(t)
                o = psum_scores(u)
                for g in range(GR):
                    mm = nc.tensor.matmul(o[:, g, :], qT[64 * e:64 * e + 64, i * GR + g, t * P:(t + 1) * P],
                                          kT[64 * e:64 * e + 64, i, 0:w], start=True, stop=True)
                mm.then_inc(sc_done, 1)

            def turn_probs(u):
                t = UNITS[u][1]
                pe.wait_ge(norm_done, GR * (u + 1))
                if u >= 1:
                    pe.wait_ge(pT_ready, u)
                pt = ps[:, 4:5 + t, :].rearrange("p b (g q) -> p (b g) q", q=P)
                for g in range(GR):
                    for kb in range(t + 1):
                        mm = nc.tensor.transpose(pt[:, g * (t + 1) + kb, :],
                                                 probs[:, u % AB, g, kb * P:(kb + 1) * P], ident[:])
                mm.then_inc(pT_turned, 1)

            def values(u):
                n, t = UNITS[u]
                pe.wait_ge(pT_ready, u + 1)
                if u >= 2:
                    pe.wait_ge(o_lo, u - 1)
                for g in range(GR):
                    r = 64 * (g % 2)
                    o = ps[r:r + 64, 6 + u % 2, (g // 2) * P:(g // 2 + 1) * P]
                    for kb in range(t + 1):
                        mm = nc.tensor.matmul(o, v_tok[:, kb, n * HD:(n + 1) * HD],
                                              probsT[:, u % AB, g * (t + 1) + kb, :], start=(kb == 0),
                                              stop=(kb == t))
                mm.then_inc(o_done, 1)

            for u in range(3):
                score(u)
            for u in range(len(UNITS) + 1):
                if u < len(UNITS):
                    turn_probs(u)
                if u + 3 < len(UNITS):
                    score(u + 3)
                if u >= 1:
                    values(u - 1)
            pe.wait_ge(o_lo, len(UNITS))
            halves(pe, "wo", hT, KD, norms[0].summed, norms[0].bank_done)

            def banks_free(free):
                return lambda g, b: pe.wait_ge(free, g * 2 + 2)
            groups(pe, "up0", KF // 2, turn_pe(pe, 0), banks_free(ffn[0].free))
            pe.wait_ge(ffn[0].free, 4 + KF - 2)
            halves(pe, "down0", hT, KF, norms[1].summed, norms[1].bank_done, (ffn[0].lo, 1))

            def cin_start(g, b):
                if isinstance(g, int):
                    pe.wait_ge(cin.free, 2 * b + 2)
                else:
                    pe.wait_ge(glu_done, g)
                    pe.wait_ge(cin.taps, (g - 2) * NS + (SUM_STEP + 2))

            def cin_taps(bank, src, matrices):
                for n, (m, j) in enumerate(matrices):
                    o = ps[:, bank, 0:T]
                    hi, lo = src[:, 0, j:j + T], src[:, 1, j:j + T]
                    nc.tensor.matmul(o, m[:, 0], hi, start=(n == 0), stop=False)
                    nc.tensor.matmul(o, m[:, 0], lo, start=False, stop=False)
                    mm = nc.tensor.matmul(o, m[:, 1], hi, start=False, stop=(n == len(matrices) - 1))
                mm.then_inc(pe_taps_done, 1)

            def own(b):
                return [(diag[:, b, i], DVE_TAPS + i) for i in range(PE_TAPS)]

            def cin_middle(g, b):
                pe.wait_ge(diag_ready, g * (2 * PE_TAPS))
                pe.wait_ge(glu_lo, g + 1)
                cin_taps(4 * (1 - b), glu_split, own(1 - b))
            groups(pe, "w_in", KD // 2, turn_pe(pe, 1), cin_start, False, cin_middle, gate_products)

            def c_turn(i):
                tok, c, bank = C_TURNED[i]
                for j in range(4):
                    mm = nc.tensor.transpose(ps[:, bank, j * P:(j + 1) * P],
                                             conv_out[:, 4 * c + j, tok * P:(tok + 1) * P], ident[:])
                mm.then_inc(c_turned, 1)
            pe.wait_ge(glu_done, KD // 2)
            pe.wait_ge(cin.taps, (KD // 2 - 2) * NS + 1)
            for i in range(3):
                c_turn(i)
            pe.wait_ge(glu_done, KD // 2 + 1)
            for i in range(3, 6):
                c_turn(i)
            pe.wait_ge(diag_ready, (KD // 2) * (2 * PE_TAPS))
            pe.wait_ge(last_diag_ready, 2 * LAST_TAPS)
            pe.wait_ge(cin.taps, (KD // 2 - 2) * NS + SUM_STEP + 2)
            pe.wait_ge(first_lo, 1)
            cin_taps(0, first_split, [(last_diag[:, i], CW - LAST_TAPS + i) for i in range(DVE_TAPS, LAST_TAPS)])
            pe.wait_ge(glu_lo, KD // 2 + 1)
            cin_taps(4, glu_split, [(last_diag[:, j], j) for j in range(DVE_TAPS)] + own(1))
            pe.wait_ge(c_stats, 1)
            pe.wait_ge(cin.taps, (KD // 2 - 1) * NS + len(LAST_STEPS) + 1)
            pe.wait_ge(last_tile_out, 1)
            for i in range(6, 8):
                c_turn(i)
            pe.wait_ge(c_shift, 1)
            for i, col in enumerate((rstd[:, 0], shift[:])):
                for tok in range(TT):
                    mm = nc.tensor.matmul(ps[:, 4, i * T + tok * P:i * T + (tok + 1) * P],
                                          col[:, tok:tok + 1].broadcast_to([P, P]), ident[:], start=True, stop=True)
            mm.then_inc(c_bcast, 1)
            halves(pe, "w_out", hT, KD, norms[2].summed, norms[2].bank_done, (s_lo, 0))
            pe.wait_ge(c_norm, KD // 2)
            groups(pe, "up1", KF // 2, turn_pe(pe, 2), banks_free(ffn[1].free))
            pe.wait_ge(ffn[1].free, 4 + KF - 2)
            halves(pe, "down1", hT, KF, norms[3].summed, norms[3].bank_done, (ffn[1].lo, 1))


def ARENA_START(nc, arena):
    return 16512


_INS = ["x", "attn_wq", "attn_wk", "attn_wv", "attn_wo", "attn_sinks", "conv_w_in", "conv_dw", "conv_norm_g",
        "conv_norm_b", "conv_w_out", "ffn_w_up", "ffn_dw", "ffn_w_down", "norm_g", "norm_b"]


def rope_table():
    inv = np.float32(500000.0) ** (-np.arange(0, ROT, 2, dtype=np.float32) / np.float32(ROT))
    ang = np.arange(T, dtype=np.float32)[:, None] * inv.astype(np.float32)[None, :]
    c, s = np.cos(ang).astype(np.float32), np.sin(ang).astype(np.float32)
    return np.ascontiguousarray(np.concatenate([c, c, -s, s], axis=1))


def kernel(**inputs):
    import numpy as _np
    import concourse.bacc as _bacc
    from concourse import mybir as _mybir
    from concourse.bass_utils import run_bass_kernel_spmd as _run

    nc = _bacc.Bacc("TRN2", target_bir_lowering=False, num_devices=1)
    arrays, args = {}, []
    for name in _INS:
        a = _np.ascontiguousarray(inputs[name])
        arrays[f"in_{name}_dram"] = a
        args.append(nc.dram_tensor(f"in_{name}_dram", a.shape, _mybir.dt.from_np(a.dtype), kind="ExternalInput").ap())
    table = rope_table()
    arrays["rope_dram"] = table
    args.append(nc.dram_tensor("rope_dram", table.shape, _mybir.dt.from_np(table.dtype), kind="ExternalInput").ap())
    args.append(nc.dram_tensor("out_dram", (1, T, D), _mybir.dt.from_np(_np.dtype("float32")),
                               kind="ExternalOutput").ap())
    trunk(nc, *args)
    r = _run(nc, [arrays], core_ids=[0])
    return r.results[0]["out_dram"]
```
